# Optimizing a Trainium2 kernel written in Bass

```python
import functools
import jax, jax.numpy as jnp
from jax import lax
import numpy as np

D_MODEL = 1024
BATCH = 1
SEQ = 1024
DEPTH = 1
DEC_BATCH = 8
DEC_SEQ = 8
PAST_LEN = 4096
PAGE_SIZE = 128

POOL_WIDTH = D_MODEL // 2
POOL_WINDOWS = (2, 4, 8, 16)
N_POOL_GROUPS = len(POOL_WINDOWS)
POOL_GROUP = POOL_WIDTH // N_POOL_GROUPS
POOL_STATE = max(POOL_WINDOWS) - 1
HEAD_DIM = 64
N_HEADS = (D_MODEL // 2) // HEAD_DIM
N_KV_HEADS = 2
GQA_GROUP = N_HEADS // N_KV_HEADS
WINDOW = 128
BLOCK = WINDOW
KV_BUF = min(WINDOW, PAST_LEN)
ATTN_WIDTH = N_HEADS * HEAD_DIM
KV_WIDTH = N_KV_HEADS * HEAD_DIM
ATTN_SCALE = HEAD_DIM ** -0.5
N_BRANCHES = 2
IN_WIDTH = POOL_WIDTH + ATTN_WIDTH + 2 * KV_WIDTH + N_BRANCHES * D_MODEL
SPLITS = (POOL_WIDTH, POOL_WIDTH + ATTN_WIDTH, POOL_WIDTH + ATTN_WIDTH + KV_WIDTH,
          POOL_WIDTH + ATTN_WIDTH + 2 * KV_WIDTH)
D_FF = 2816
CONV_WIDTH = 3
CONV_STATE = CONV_WIDTH - 1
EPS = 1e-6

kernel_name = "hybrid_pool_swa_sink_convffn_step"

def rmsnorm(x, g):
    xf = x.astype(jnp.float32)
    inv = lax.rsqrt(jnp.mean(xf * xf, axis=-1, keepdims=True) + EPS)
    return (xf * inv).astype(x.dtype) * g

def pool_mix(u, prefix, pos0, w_pool_grp, pool_scale):
    B, T, _ = u.shape
    ext = jnp.concatenate([prefix, u], axis=1).astype(jnp.float32)
    cs = jnp.concatenate([jnp.zeros((B, 1, POOL_WIDTH), jnp.float32),
                          jnp.cumsum(ext, axis=1)], axis=1)
    end = cs[:, POOL_STATE + 1:]
    pos = pos0 + jnp.arange(T)
    outs = []
    for g, w in enumerate(POOL_WINDOWS):
        sl = slice(g * POOL_GROUP, (g + 1) * POOL_GROUP)
        start = cs[:, POOL_STATE + 1 - w:POOL_STATE + 1 - w + T, sl]
        cnt = jnp.minimum(pos + 1, w).astype(jnp.float32)[None, :, None]
        outs.append((end[..., sl] - start) / cnt - ext[:, POOL_STATE:, sl])
    d = jnp.stack(outs, axis=2).astype(u.dtype)
    y = jnp.einsum('btgc,gcd->btgd', d, w_pool_grp).reshape(B, T, POOL_WIDTH)
    return y * pool_scale

def sink_softmax(s, mask, sinks):
    s = jnp.where(mask, s, -jnp.inf)
    sk = jnp.broadcast_to(sinks.astype(jnp.float32).reshape(N_KV_HEADS, GQA_GROUP, 1, 1),
                          s.shape[:-1] + (1,))
    p = jax.nn.softmax(jnp.concatenate([s, sk], axis=-1), axis=-1)
    return p[..., :-1]

def attn_prompt(q, k, v, sinks):
    B, T = q.shape[:2]
    NB = T // BLOCK
    qb = q.reshape(B, NB, BLOCK, N_KV_HEADS, GQA_GROUP, HEAD_DIM)
    kb = k.reshape(B, NB, BLOCK, N_KV_HEADS, HEAD_DIM)
    vb = v.reshape(B, NB, BLOCK, N_KV_HEADS, HEAD_DIM)
    kk = jnp.concatenate([jnp.concatenate([jnp.zeros_like(kb[:, :1]), kb[:, :-1]], axis=1), kb], axis=2)
    vv = jnp.concatenate([jnp.concatenate([jnp.zeros_like(vb[:, :1]), vb[:, :-1]], axis=1), vb], axis=2)
    s = jnp.einsum('bnqkgd,bnskd->bnkgqs', qb, kk).astype(jnp.float32) * ATTN_SCALE
    i = jnp.arange(BLOCK)[:, None]
    j = jnp.arange(2 * BLOCK)[None, :]
    diff = i + BLOCK - j
    band = (diff >= 0) & (diff <= WINDOW)
    key_ok = (jnp.arange(NB)[:, None, None] * BLOCK - BLOCK + j[None]) >= 0
    mask = (band[None] & key_ok)[None, :, None, None]
    p = sink_softmax(s, mask, sinks).astype(v.dtype)
    o = jnp.einsum('bnkgqs,bnskd->bnqkgd', p, vv).reshape(B, T, ATTN_WIDTH)
    return o, k[:, -KV_BUF:], v[:, -KV_BUF:]

def attn_sample(q, k, v, sinks, cache_k, cache_v):
    B, T = q.shape[:2]
    kk = jnp.concatenate([cache_k, k], axis=1)
    vv = jnp.concatenate([cache_v, v], axis=1)
    qg = q.reshape(B, T, N_KV_HEADS, GQA_GROUP, HEAD_DIM)
    s = jnp.einsum('bqkgd,bskd->bkgqs', qg, kk).astype(jnp.float32) * ATTN_SCALE
    diff = jnp.arange(T)[:, None] + KV_BUF - jnp.arange(KV_BUF + T)[None, :]
    mask = ((diff >= 0) & (diff <= WINDOW))[None, None, None]
    p = sink_softmax(s, mask, sinks).astype(v.dtype)
    o = jnp.einsum('bkgqs,bskd->bqkgd', p, vv).reshape(B, T, ATTN_WIDTH)
    return o, kk[:, -KV_BUF:], vv[:, -KV_BUF:]

def conv_ffn(x, prefix, g_ffn, w_up, conv_w, conv_b, w_down):
    h = rmsnorm(x, g_ffn)
    up = h @ w_up
    ext = jnp.concatenate([prefix, up], axis=1)
    c = lax.conv_general_dilated(ext, conv_w[:, None, :].astype(ext.dtype), window_strides=(1,),
                                 padding='VALID', dimension_numbers=('NWC', 'WIO', 'NWC'),
                                 feature_group_count=2 * D_FF) + conv_b
    gate, val = jnp.split(c, 2, axis=-1)
    return (jax.nn.silu(gate) * val) @ w_down, ext[:, -CONV_STATE:]

def layer(x, pool_prefix, pos0, attend, conv_prefix, g_mix, w_in, w_pool_grp, pool_scale, sinks,
          w_branch_pool, w_branch_attn, w_out, g_ffn, w_up, conv_w, conv_b, w_down):
    B, T, _ = x.shape
    h = rmsnorm(x, g_mix)
    z = h @ w_in
    u, q, k, v, gl = jnp.split(z, SPLITS, axis=-1)
    a = pool_mix(u, pool_prefix, pos0, w_pool_grp, pool_scale)
    o, k_state, v_state = attend(q.reshape(B, T, N_HEADS, HEAD_DIM),
                                 k.reshape(B, T, N_KV_HEADS, HEAD_DIM),
                                 v.reshape(B, T, N_KV_HEADS, HEAD_DIM), sinks)
    ga, gb = jnp.split(jax.nn.sigmoid(gl), N_BRANCHES, axis=-1)
    mixed = ga * (a @ w_branch_pool) + gb * (o @ w_branch_attn)
    x = x + mixed @ w_out
    f, conv_state = conv_ffn(x, conv_prefix, g_ffn, w_up, conv_w, conv_b, w_down)
    x = x + f
    pool_state = jnp.concatenate([pool_prefix, u], axis=1)[:, -POOL_STATE:]
    return x, pool_state, k_state, v_state, conv_state

def setup_inputs(seed: int = 0) -> dict:
    key = jax.random.key(seed)
    ks = jax.random.split(key, 20)

    def nrm(k, shape, scale):
        return jax.random.normal(k, shape, jnp.float32) * scale

    return {
        "x_prompt": nrm(ks[0], (BATCH, SEQ, D_MODEL), 1.0),
        "x_sample": nrm(ks[1], (DEC_BATCH, DEC_SEQ, D_MODEL), 1.0),
        "state_pool": nrm(ks[2], (DEPTH, DEC_BATCH, POOL_STATE, POOL_WIDTH), 1.0),
        "cache_k": nrm(ks[3], (DEPTH, DEC_BATCH, KV_BUF, N_KV_HEADS, HEAD_DIM), 1.0),
        "cache_v": nrm(ks[4], (DEPTH, DEC_BATCH, KV_BUF, N_KV_HEADS, HEAD_DIM), 1.0),
        "state_conv": nrm(ks[5], (DEPTH, DEC_BATCH, CONV_STATE, 2 * D_FF), 1.0),
        "g_mix": 1.0 + nrm(ks[6], (DEPTH, D_MODEL), 0.02),
        "w_in": nrm(ks[7], (DEPTH, D_MODEL, IN_WIDTH), D_MODEL ** -0.5),
        "w_pool_grp": nrm(ks[8], (DEPTH, N_POOL_GROUPS, POOL_GROUP, POOL_GROUP), POOL_GROUP ** -0.5),
        "pool_scale": 1.0 + nrm(ks[9], (DEPTH, POOL_WIDTH), 0.02),
        "sinks": nrm(ks[10], (DEPTH, N_HEADS), 0.5),
        "w_branch_pool": nrm(ks[11], (DEPTH, POOL_WIDTH, D_MODEL), POOL_WIDTH ** -0.5),
        "w_branch_attn": nrm(ks[12], (DEPTH, ATTN_WIDTH, D_MODEL), ATTN_WIDTH ** -0.5),
        "w_out": nrm(ks[13], (DEPTH, D_MODEL, D_MODEL), D_MODEL ** -0.5),
        "g_ffn": 1.0 + nrm(ks[14], (DEPTH, D_MODEL), 0.02),
        "w_up": nrm(ks[15], (DEPTH, D_MODEL, 2 * D_FF), D_MODEL ** -0.5),
        "conv_w": nrm(ks[16], (DEPTH, CONV_WIDTH, 2 * D_FF), CONV_WIDTH ** -0.5),
        "conv_b": nrm(ks[17], (DEPTH, 2 * D_FF), 0.01),
        "w_down": nrm(ks[18], (DEPTH, D_FF, D_MODEL), D_FF ** -0.5),
        "g_final": 1.0 + nrm(ks[19], (D_MODEL,), 0.02),
    }

def reference(x_prompt, x_sample, state_pool, cache_k, cache_v, state_conv, g_mix, w_in,
              w_pool_grp, pool_scale, sinks, w_branch_pool, w_branch_attn, w_out, g_ffn,
              w_up, conv_w, conv_b, w_down, g_final):
    yp, ys = x_prompt, x_sample
    pool_p, k_p, v_p, conv_p = [], [], [], []
    pool_s, k_s, v_s, conv_s = [], [], [], []
    for l in range(DEPTH):
        lw = (g_mix[l], w_in[l], w_pool_grp[l], pool_scale[l], sinks[l], w_branch_pool[l],
              w_branch_attn[l], w_out[l], g_ffn[l], w_up[l], conv_w[l], conv_b[l], w_down[l])
        zp = jnp.zeros((yp.shape[0], POOL_STATE, POOL_WIDTH), yp.dtype)
        zc = jnp.zeros((yp.shape[0], CONV_STATE, 2 * D_FF), yp.dtype)
        yp, a1, a2, a3, a4 = layer(yp, zp, 0, attn_prompt, zc, *lw)
        pool_p.append(a1); k_p.append(a2); v_p.append(a3); conv_p.append(a4)
        att = functools.partial(attn_sample, cache_k=cache_k[l], cache_v=cache_v[l])
        ys, b1, b2, b3, b4 = layer(ys, state_pool[l], PAST_LEN, att, state_conv[l], *lw)
        pool_s.append(b1); k_s.append(b2); v_s.append(b3); conv_s.append(b4)
    yp = rmsnorm(yp, g_final)
    ys = rmsnorm(ys, g_final)
    return (yp, ys, jnp.stack(pool_p), jnp.stack(k_p), jnp.stack(v_p), jnp.stack(conv_p),
            jnp.stack(pool_s), jnp.stack(k_s), jnp.stack(v_s), jnp.stack(conv_s))


_drawn_inputs = setup_inputs


def setup_inputs(seed=0):
    import zlib

    import numpy as np

    out = dict(_drawn_inputs(seed))
    spreads = {}
    factors = {'g_mix': 2.736,
     'pool_scale': 6.08,
     'sinks': 56.119,
     'g_ffn': 7.938,
     'conv_b': 21.942,
     'g_final': 8.091}
    for name, (base, spread) in spreads.items():
        noise = np.random.default_rng([zlib.crc32(name.encode()), seed]).standard_normal(out[name].shape)
        drawn = base * np.exp(spread * noise) if base else spread * noise
        out[name] = __import__('jax').numpy.asarray(drawn.astype(out[name].dtype))
    for name, factor in factors.items():
        out[name] = (out[name] * factor).astype(out[name].dtype)
    return out
```

```python
from contextlib import ExitStack

import concourse.bass as bass
from concourse import mybir

F32 = mybir.dt.float32
F32R = mybir.dt.float32r
ALU = mybir.AluOpType
ACT = mybir.ActivationFunctionType
AX = mybir.AxisListType

P = 128
D = 1024
SEQ = 1024
DEC_B, DEC_T = 8, 8
NSAMP = DEC_B * DEC_T
T = SEQ + NSAMP
NP = 364
TP = 3 * NP
KD = D // P
PADS = slice(T, TP)

POOL_W = D // 2
NG = 4
PSTATE = 15
UEXT = PSTATE + SEQ + DEC_B * (PSTATE + DEC_T)
USAMP = PSTATE + SEQ

HD = 64
NQ = 4
WIN = 128
NBLK = SEQ // WIN
SCALE = HD ** -0.5
MASKED = -1e30
SKEYS = WIN + DEC_T

D_FF = 2816
NFF = D_FF // P
CSTATE = 2
ESAMP = CSTATE + SEQ
EXT = ESAMP + DEC_B * (CSTATE + DEC_T)
NCONV = EXT - 2
EPS = 1e-6

NTILE = 9
TILE_ROWS = [P] * (SEQ // P) + [NSAMP]

N_U, N_Q = 4, 4
CHUNK_K, CHUNK_V, CHUNK_GATE = 8, 9, 10
CHUNK_BRANCH = CHUNK_GATE + 16
CHUNK_OUT = CHUNK_BRANCH + KD
CHUNK_UP = CHUNK_OUT + KD
N_CHUNKS = CHUNK_UP + 2 * NFF

ENTRIES = ([("u", g) for g in range(4)] + [("q", 0), ("q", 1), ("pool", 0), ("q", 2), ("pool", 1), ("q", 3),
           ("k", 0), ("pool", 2), ("v", 0), ("pool", 3)])
FIRST_CHUNK = {"u": 0, "q": 4, "k": 8, "v": 9}
FILL_GATE = len(ENTRIES)
FILL_BRANCH = FILL_GATE + 16
FILL_OUT = FILL_BRANCH + 2 * KD
FILL_FFN = FILL_OUT + KD

AUX_CONST, AUX_CONV, AUX_POOL, AUX_KC, AUX_U, AUX_K, AUX_V, AUX_VNEW = range(8)
AUX_S0 = 8


def aux_scores(s):
    return {0: 8, 1: 14, 2: 20}[s] if isinstance(s, int) and s < 3 else s * 3 + 14


def aux_turn(s):
    return {0: 10, 1: 16}[s] if isinstance(s, int) and s < 2 else s * 3 + 15


def aux_values(s):
    return {0: 11, 1: 17}[s] if isinstance(s, int) and s < 2 else s * 3 + 16


AUX_SAMPLE = [(9, 12, 13), (15, 18, 19)]
AUX_X = 3 * 15 + 17
AUX_SSQ = AUX_X + 2 * KD
AUX_TAIL = AUX_SSQ + 1
AUX_Y = AUX_TAIL + 2 * NFF
AUX_SSQ2 = AUX_Y + 2 * KD


def landed(pair):
    return pair * 24 + 48


class Chain:

    def __init__(self, eng, sem):
        self.eng, self.sem, self.n = eng, sem, 0

    def link(self, ins):
        ins.then_inc(self.sem, 1)
        self.n = self.n + 1
        self.eng.wait_ge(self.sem, self.n)

    def enter(self, i, per):
        self.start, self.n, self.local = self.n, i * per + self.n, self.n

    def leave(self, times, per):
        self.n = self.start + times * per


def hybrid_layer(nc, x_prompt, x_sample, state_pool, cache_k, cache_v, state_conv, g_mix, w_in, w_pool_grp,
                 pool_scale, sinks, w_branch_pool, w_branch_attn, w_out, g_ffn, w_up, conv_w, conv_b, w_down,
                 g_final, y_prompt, y_sample, pool_prompt, k_prompt, v_prompt, conv_prompt,
                 pool_sample, k_sample, v_sample, conv_sample):
    x_p = x_prompt[0]
    x_s = x_sample.rearrange("b t d -> (b t) d")
    x_tiles = [x_p[j * P:(j + 1) * P] for j in range(NTILE - 1)] + [x_s]
    y_s = y_sample.rearrange("b t d -> (b t) d")
    y_tiles = [y_prompt[0][j * P:(j + 1) * P] for j in range(NTILE - 1)] + [y_s]
    win_v = w_in[0].rearrange("(k p) n -> p k n", p=P)
    wout_v = w_out[0].rearrange("(k p) n -> p k n", p=P)
    wup_v = w_up[0].rearrange("(k p) n -> p k n", p=P)
    wbp_v = w_branch_pool[0].rearrange("(k p) n -> p k n", p=P)
    wba_v = w_branch_attn[0].rearrange("(v c d) n -> v d c n", v=2, c=NQ)
    wdn_v = w_down[0].rearrange("(i k p) n -> p i k n", p=P, k=2)
    gates_dram = nc.dram_tensor("gates_scratch", [16, P, TP], F32).ap()

    with ExitStack() as ctx:
        free_at = [(nc.sbuf_base + 63) // 64 * 64]
        top = nc.sbuf_usable_end

        def region(nbytes):
            start = free_at[0]
            free_at[0] += (nbytes + 31) // 32 * 32
            assert free_at[0] <= top, (free_at[0], top)
            return start

        class Place:

            def __init__(self, start, size):
                self.at, self.end = start, start + size

            def __call__(self, name, shape, dt=F32):
                n = 4
                for d in shape[1:]:
                    n *= d
                t = nc.alloc_sbuf_tensor_at(name, [P] + shape[1:], dt, offset=self.at)
                self.at += (n + 31) // 32 * 32
                assert self.at <= self.end, (name, self.at - self.end)
                return t

        ROW = TP * 4
        REG_H = region(16 * ROW)
        REG_M = region(16 * ROW)
        REG_UP = region(16384)
        REG_RAW = region(8192)
        REG_DN = region(24576)
        REG_MISC = region(22400)

        at = Place(REG_UP, 16384)
        up_hi = at("up_hi", [P, 2, KD, P], F32R)
        up_lo = at("up_lo", [P, 2, KD, P], F32R)
        at = Place(REG_UP, 16384)
        sq2 = at("sq2", [P, TP])
        sqsum2 = at("sqsum2", [P, TP])
        raw = Place(REG_RAW, 8192)("raw", [P, 2, KD, P])
        at = Place(REG_DN, 24576)
        dn_hi = at("dn_hi", [P, 2, D], F32R)
        dn_lo = at("dn_lo", [P, 2, D], F32R)
        raw_dn = at("raw_dn", [P, 2, D])

        at = Place(REG_MISC, 22400)
        ident = at("ident", [P, P])
        ones = at("ones", [P, P])
        mask = at("mask", [P, 2 * WIN])
        mask_first = at("mask_first", [P, 2 * WIN])
        smask = at("smask", [P, SKEYS])
        cols = at("cols", [P, 4 * 2 * NFF + KD + NG])
        cw = cols[:, 0:8 * NFF].rearrange("p (a c) -> p a c", a=4)
        gffn = cols[:, 8 * NFF:8 * NFF + KD]
        pscale = cols[:, 8 * NFF + KD:8 * NFF + KD + NG]
        cstate = at("cstate", [P, 2 * NFF, DEC_B * CSTATE])
        rcount = at("rcount", [P, 16])
        sink_b = at("sink_b", [P, 8])
        sink_s = at("sink_s", [P, 2])
        sink_t = at("sink_t", [P, 2])
        ssq = at("ssq", [P, NTILE])
        root = at("root", [P, NTILE])
        rstd = at("rstd", [P, NTILE])
        smx = at("smx", [P, 4])
        snegm = at("snegm", [P, 4])
        ssum = at("ssum", [P, 4])
        sesink = at("sesink", [P, 4])
        sden = at("sden", [P, 4])
        srec = at("srec", [P, 4])
        wgrp = at("wgrp", [P, NG, P])
        vnew = at("vnew", [P, DEC_B, P])
        qblk_at = at.at
        qblk = at("qblk", [P, NQ, WIN])
        upack = at("upack", [P, NG, NSAMP])
        qpack = at("qpack", [P, DEC_B, NQ, DEC_T])
        tpack = at("tpack", [P, 2, CSTATE + 2 * DEC_B])
        x4_at = at.at

        tmp = Place(qblk_at, 2048)
        rep8 = tmp("rep8", [P, 16, 8])
        rep4 = tmp("rep4", [P, 4, 4, 8])
        mask8 = tmp("mask8", [P, SKEYS])
        tmp = Place(x4_at, 4608)
        sprob = tmp("sprob", [P, 2, SKEYS])
        sprob_c = tmp("sprob_c", [P, 2, P])
        sprob_n = tmp("sprob_n", [P, 2, P])
        xcol1 = Place(x4_at, 4608)("xcol1", [P, NTILE, P])
        diag = Place(x4_at, 4608)("diag", [P, NTILE, P])
        conv_val = Place(x4_at, 4608)("conv_val", [P, EXT])

        at = Place(REG_H, 16 * ROW)
        h_hi = at("h_hi", [P, KD, TP], F32R)
        h_lo = at("h_lo", [P, KD, TP], F32R)
        at = Place(REG_H, 16 * ROW)
        ao_hi = at("ao_hi", [P, KD, TP], F32R)
        ao_lo = at("ao_lo", [P, KD, TP], F32R)
        at = Place(REG_H, 16 * ROW)
        y = at("y", [P, KD, TP])
        act_at = at.at
        act_hi = at("act_hi", [P, 2, TP], F32R)
        act_lo = at("act_lo", [P, 2, TP], F32R)
        ext_gate = at("ext_gate", [P, EXT])
        ext_val = at("ext_val", [P, EXT])
        conv_gate = at("conv_gate", [P, EXT])
        tail_rows = at("tail_rows", [P, 2, 2, P])
        at = Place(act_at, 4 * ROW)
        xsq = at("xsq", [P, 4, TP])
        xT, sq, sqsum = xsq[:, 0:2], xsq[:, 2], xsq[:, 3]

        at = Place(REG_M, 16 * ROW)
        xtok = at("xtok", [P, NTILE, D])
        at = Place(REG_M, 16 * ROW)
        uext = at("uext", [P, NG, UEXT])
        qT = at("qT", [P, NQ, TP])
        kT = at("kT", [P, WIN + TP])
        vT_at = at.at
        vT = at("vT", [P, TP])
        gmix_b = Place(vT_at, ROW)("gmix_b", [P, D])
        vtok_at = at.at
        vtok = at("vtok", [P, 1 + NBLK, P])
        cst = Place(vtok_at, 4608)("cst", [P, 6, P])
        kcT_at = at.at
        kcT = at("kcT", [P, DEC_B, WIN])
        sq_junk = Place(kcT_at, 4096)("sq_junk", [P, D])
        vc = at("vc", [P, DEC_B, P])
        prob_at = at.at
        prob = at("prob", [P, NQ, 2 * WIN])
        probT_at = at.at
        probT = at("probT", [P, 2, NQ * P])
        kblk = at("kblk", [P, 2 * WIN])
        vblk_at = at.at
        vblk = at("vblk", [P, 2, P])
        pst = Place(prob_at, 4096)("pst", [P, POOL_W])
        tmp = Place(prob_at, 4096)
        uout_p = tmp("uout_p", [P, POOL_W])
        uout_s = tmp("uout_s", [P, POOL_W])
        ktok = Place(probT_at, 4096)("ktok", [P, DEC_B, P])
        tmp = Place(probT_at, 4096)
        kout_p = tmp("kout_p", [P, P])
        kout_s = tmp("kout_s", [P, P])
        at = Place(REG_M, 16 * ROW)
        mx_hi = at("mx_hi", [P, KD, TP], F32R)
        mx_lo = at("mx_lo", [P, KD, TP], F32R)
        at = Place(REG_M, 16 * ROW)
        h2_hi = at("h2_hi", [P, KD, TP], F32R)
        h2_lo = at("h2_lo", [P, KD, TP], F32R)
        at = Place(REG_M, 16 * ROW)
        ytok = at("ytok", [P, NTILE, D])
        gfin_b = at("gfin_b", [P, D])

        convst = Place(REG_DN, 24576)("convst", [P, 2 * D_FF])
        at = Place(REG_DN, 24576)
        sum_a = at("sum_a", [P, UEXT])
        sum_b = at("sum_b", [P, UEXT])
        dT = at("dT", [P, TP])
        gate_st = at("gate_st", [P, 2, TP])
        at = Place(REG_DN, 24576)
        gates = at("gates", [P, 2, 2, TP])
        xcol0 = at("xcol0", [P, NTILE, P])
        xcol = [xcol0, xcol1]

        PS = ctx.enter_context(nc.psum_tensor("PS", [P, 8, 512], F32))
        acc = [PS[:, 3 * s:3 * s + 3, 0:NP] for s in range(2)]
        aux = PS[:, 6:8, :].rearrange("p b n -> p (b n)")
        bcast = PS[:, 0:3, :].rearrange("p b n -> p (b n)")[:, 0:TP]

        def sem(name):
            return ctx.enter_context(nc.semaphore(name))

        x_in = [sem(f"x_in{j}") for j in range(NTILE)]
        gmix_in, const_in, convst_in = sem("gmix_in"), sem("const_in"), sem("convst_in")
        raw_in = [sem("raw_in0"), sem("raw_in1")]
        dn_in = sem("dn_in")
        wgrp_in = sem("wgrp_in")
        u_out, kv_out = sem("u_out"), sem("kv_out")
        dram_copy = sem("dram_copy")
        gate_out = [sem("gate_out0"), sem("gate_out1")]
        gate_in = [sem("gate_in0"), sem("gate_in1")]
        xcol_in = [sem("xcol_in0"), sem("xcol_in1")]
        tail_out = sem("tail_out")
        gfin_in = sem("gfin_in")
        y_out = sem("y_out")
        xt_full, acc_full, aux_full, bc_full = sem("xt_full"), sem("acc_full"), sem("aux_full"), sem("bc_full")
        x_sq, x_root, x_hi = sem("x_sq"), sem("x_root"), sem("x_hi")
        w_hi, dn_hi_done = sem("w_hi"), sem("dn_hi_done")
        proj_done, exp_done, sexp_done = sem("proj_done"), sem("exp_done"), sem("sexp_done")
        ao_hi_done, mix_hi_done = sem("ao_hi_done"), sem("mix_hi_done")
        sq_done, root2, h2_hi_done = sem("sq_done"), sem("root2"), sem("h2_hi_done")
        ext_done, silu_done, act_hi_done = sem("ext_done"), sem("silu_done"), sem("act_hi_done")
        x_ms, x_scaled, x_lo = sem("x_ms"), sem("x_scaled"), sem("x_lo")
        w_lo, dn_lo_done = sem("w_lo"), sem("dn_lo_done")
        d_done, smax_done, prob_done, ssmax_done, sprob_done = (sem("d_done"), sem("smax_done"), sem("prob_done"),
                                                                sem("ssmax_done"), sem("sprob_done"))
        acc_free = sem("acc_free")
        aux_free = sem("aux_free")
        ao_lo_done, mix_sum, mix_lo_done = sem("ao_lo_done"), sem("mix_sum"), sem("mix_lo_done")
        ms2, diag_done, h2_sum, h2_lo_done = sem("ms2"), sem("diag_done"), sem("h2_sum"), sem("h2_lo_done")
        conv_done, prod_done, act_lo_done = sem("conv_done"), sem("prod_done"), sem("act_lo_done")
        y_scaled = sem("y_scaled")
        dve_step = sem("dve_step")
        pool_step, const_done, uzero_done = sem("pool_step"), sem("const_done"), sem("uzero_done")
        qk_staged, v_staged, sq_added, pads_done = (sem("qk_staged"), sem("v_staged"), sem("sq_added"),
                                                               sem("pads_done"))
        u_packed = sem("u_packed")

        block = ctx.enter_context(nc.Block())

        def samples(t, first, width):
            skip = width - DEC_T
            return t[:, first:first + DEC_B * width].rearrange("p (b w) -> p b w", b=DEC_B)[:, :, skip:width]

        def split_source(c):
            return raw[:, c % 2], up_hi[:, c % 2], up_lo[:, c % 2]

        @block.sync
        def _(sp):
            def load_chunk(c, half, views, wait=True):
                if wait:
                    sp.wait_ge(w_lo, c - 1)
                for n, (dst, src) in enumerate(views):
                    last = n == len(views) - 1
                    sp.dma_start(dst, src).then_inc(raw_in[half], 48 - 16 * n if last else 16)

            def in_views(c):
                r = raw[:, c % 2]
                if N_U <= c < N_U + N_Q:
                    base = POOL_W + (c - N_U) * HD
                    return [(r[:, :, v * HD:(v + 1) * HD], win_v[:, :, base + v * NQ * HD:base + v * NQ * HD + HD])
                            for v in range(2)]
                col = c * P if c < N_U else 2 * POOL_W + (c - CHUNK_K) * P
                return [(r, win_v[:, :, col:col + P])]

            def gate_views(cg, half):
                col = cg * P + (2 * POOL_W + 2 * P)
                return [(raw[:, half], win_v[:, :, bass.ds(col, P)])]

            def branch_views(m, half):
                r = raw[:, half]
                c = bass.ds(m * P, P)
                return [(r[:, 0:4], wbp_v[:, :, c])] + [(r[v * HD:(v + 1) * HD, 4:8], wba_v[v][:, :, c]) for v in range(2)]

            def out_views(m, half):
                return [(raw[:, half], wout_v[:, :, bass.ds(m * P, P)])]

            def up_views(j, val):
                return [(raw[:, val], wup_v[:, :, bass.ds(j * P + val * D_FF, P)])]

            def load_x(j):
                sp.dma_start(xtok[0:TILE_ROWS[j], j, :], x_tiles[j]).then_inc(x_in[j], 16)

            load_x(0)
            sp.dma_start(gmix_b[:, :], g_mix.partition_broadcast(P).rearrange("p a d -> p (a d)")).then_inc(gmix_in, 16)
            load_x(1)
            load_x(2)
            load_chunk(0, 0, in_views(0), wait=False)
            for j in range(3, NTILE):
                load_x(j)
            load_chunk(1, 1, in_views(1), wait=False)
            cwv = conv_w[0].rearrange("a (c p) -> c a p", p=P)
            sp.dma_start(cst[0:2 * NFF, 0:3, :], cwv).then_inc(const_in, 16)
            sp.dma_start(cst[0:2 * NFF, 3, :], conv_b[0].rearrange("(c p) -> c p", p=P)).then_inc(const_in, 16)
            sp.dma_start(cst[0:KD, 4, :], g_ffn[0].rearrange("(c p) -> c p", p=P)).then_inc(const_in, 16)
            sp.dma_start(cst[0:NG, 5, :], pool_scale[0].rearrange("(c p) -> c p", p=P)).then_inc(const_in, 16)
            sp.dma_start(sink_b[:, :], sinks.partition_broadcast(P).rearrange("p a d -> p (a d)")).then_inc(const_in, 16)
            with nc.allow_non_contiguous_dma(reason="eight sink logits"):
                sp.dma_start(sink_t[0:NQ, :], sinks[0].rearrange("(v c) -> c v", v=2)).then_inc(const_in, 16)
            sp.dma_start(convst[0:16, :], state_conv[0].rearrange("b r c -> (b r) c")).then_inc(convst_in, 16)
            sp.dma_start(pst[0:DEC_B * PSTATE, :], state_pool[0].rearrange("b r c -> (b r) c")).then_inc(const_in, 16)
            sp.dma_start(ktok[:, :, :], cache_k[0].rearrange("b t v d -> t b (v d)")).then_inc(const_in, 16)
            sp.dma_start(vc[:, :, :], cache_v[0].rearrange("b t v d -> t b (v d)")).then_inc(const_in, 16)
            sp.dma_start(wgrp[:, :, :], w_pool_grp[0].rearrange("g c d -> c g d")).then_inc(wgrp_in, 16)
            sp.dma_start(pool_sample[0][:, 0:PSTATE - DEC_T], state_pool[0][:, DEC_T:PSTATE]).then_inc(dram_copy, 16)
            sp.dma_start(k_sample[0][:, 0:WIN - DEC_T], cache_k[0][:, DEC_T:WIN]).then_inc(dram_copy, 16)
            sp.dma_start(v_sample[0][:, 0:WIN - DEC_T], cache_v[0][:, DEC_T:WIN]).then_inc(dram_copy, 16)

            for c in range(2, CHUNK_GATE):
                load_chunk(c, c % 2, in_views(c))
            for cg in range(4):
                if cg == 0:
                    sp.wait_ge(aux_free, AUX_U + 1)
                    sp.dma_start(pool_prompt[0, 0], uout_p[0:PSTATE, :]).then_inc(u_out, 16)
                    for b in range(DEC_B):
                        sp.dma_start(pool_sample[0][b, PSTATE - DEC_T:PSTATE],
                                     uout_s[b * DEC_T:(b + 1) * DEC_T, :]).then_inc(u_out, 16)
                if cg == 2:
                    sp.wait_ge(aux_free, AUX_K + 1)
                    sp.dma_start(k_prompt[0, 0].rearrange("t v d -> t (v d)"), kout_p[:, :]).then_inc(kv_out, 16)
                    for b in range(DEC_B):
                        sp.dma_start(k_sample[0][b, WIN - DEC_T:WIN].rearrange("t v d -> t (v d)"),
                                     kout_s[b * DEC_T:(b + 1) * DEC_T, :]).then_inc(kv_out, 16)
                load_chunk(CHUNK_GATE + cg, cg % 2, gate_views(cg, cg % 2))
            sp.wait_ge(aux_free, AUX_VNEW + 1)
            sp.dma_start(v_prompt[0, 0].rearrange("t v d -> t (v d)"), vtok[:, NBLK, :]).then_inc(kv_out, 16)
            sp.dma_start(v_sample[0][:, WIN - DEC_T:WIN].rearrange("b t v d -> t b (v d)"),
                         vnew[0:DEC_T, :, :]).then_inc(kv_out, 16)

            def store_gate(cg, half):
                sp.wait_ge(proj_done, cg + (FILL_GATE + 1))
                sp.dma_start(gates_dram[cg], gate_st[:, half, :]).then_inc(gate_out[half], 16)

            with sp.Fori(0, 6) as n:
                for half in range(2):
                    store_gate(n * 2 + half, half)
                    load_chunk(n * 2 + (CHUNK_GATE + 4 + half), half, gate_views(n * 2 + (4 + half), half))
            for cg in range(12, 16):
                store_gate(cg, cg % 2)
                load_chunk(CHUNK_BRANCH + cg - 12, cg % 2, branch_views(cg - 12, cg % 2))

            def load_gates(m, half):
                sp.dma_start(gates[:, half, 0, :], gates_dram[m]).then_inc(gate_in[half], 16)
                sp.dma_start(gates[:, half, 1, :], gates_dram[m + KD]).then_inc(gate_in[half], 16)

            sp.wait_ge(gate_out[0], 16 * 8)
            sp.wait_ge(gate_out[1], 16 * 8)
            load_gates(0, 0)
            load_gates(1, 1)

            def load_xcol(m, half):
                c = bass.ds(m * P, P)
                sp.dma_start(xcol[half][:, 0:NTILE - 1, :], x_p.rearrange("(j p) d -> p j d", p=P)[:, :, c])\
                    .then_inc(xcol_in[half], 16)
                sp.dma_start(xcol[half][0:NSAMP, NTILE - 1, :], x_s[:, c]).then_inc(xcol_in[half], 16)

            load_xcol(0, 0)
            load_xcol(1, 1)
            for m in range(KD):
                if m < KD - 2:
                    sp.wait_ge(mix_lo_done, m + 1)
                    load_gates(m + 2, m % 2)
                c = CHUNK_BRANCH + m + 4
                if m < 4:
                    load_chunk(c, c % 2, branch_views(m + 4, m % 2))
                else:
                    load_chunk(c, c % 2, out_views(m - 4, m % 2))
            for m in range(KD):
                if m < KD - 2:
                    sp.wait_ge(aux_full, AUX_X + 2 * m + 2)
                    load_xcol(m + 2, m % 2)
                c = CHUNK_OUT + m + 4
                if m < 4:
                    load_chunk(c, c % 2, out_views(m + 4, m % 2))
                else:
                    load_chunk(c, c % 2, up_views((m - 4) // 2, m % 2))

            def load_down(i):
                sp.dma_start(raw_dn[:, :, :], wdn_v[:, i]).then_inc(dn_in, 16)

            sp.wait_ge(mix_lo_done, KD)
            sp.wait_ge(aux_full, AUX_X + 2 * KD)
            load_down(0)

            def store_tails(i):
                sp.wait_ge(aux_free, i * 4 + (AUX_TAIL + 4))
                for v in range(2):
                    c = bass.ds(i * (2 * P) + v * D_FF, 2 * P)
                    sp.dma_start(conv_prompt[0, 0][:, c], tail_rows[0:CSTATE, v, :, :].rearrange("r e p -> r (e p)"))\
                        .then_inc(tail_out, 16)
                    sp.dma_start(conv_sample[0].rearrange("b r c -> (b r) c")[:, c],
                                 tail_rows[CSTATE:CSTATE + 16, v, :, :].rearrange("r e p -> r (e p)")).then_inc(tail_out, 16)

            with sp.Fori(0, NFF // 2 - 1) as i:
                for e in range(2):
                    for val in range(2):
                        load_chunk(i * 4 + (CHUNK_UP + 4 + 2 * e + val), val, up_views(i * 2 + (2 + e), val))
                sp.wait_ge(dn_lo_done, i + 1)
                load_down(i + 1)
                store_tails(i)
            sp.wait_ge(acc_full, FILL_FFN + 12 * (NFF // 2 - 1) + 4)
            sp.dma_start(gfin_b[:, :], g_final.partition_broadcast(P)).then_inc(gfin_in, 16)
            store_tails(NFF // 2 - 1)
            for j in range(NTILE):
                sp.wait_ge(y_scaled, j + 1)
                sp.dma_start(y_tiles[j], ytok[0:TILE_ROWS[j], j, :]).then_inc(y_out, 16)
            sp.wait_ge(dram_copy, 16 * 3)
            sp.wait_ge(u_out, 16 * 9)
            sp.wait_ge(kv_out, 16 * 11)
            sp.wait_ge(tail_out, 16 * 4 * (NFF // 2))
            sp.wait_ge(y_out, 16 * NTILE)

        @block.tensor
        def _(pe):
            def gemm(s, c, first_k, ks, rhs_hi, rhs_lo, hooks=None, ready=None):
                _, w_h, w_l = split_source(c)
                for n, k in enumerate(ks):
                    if hooks and n in hooks:
                        hooks[n]()
                    if ready:
                        ready(k)
                    for q, (w, x) in enumerate(((w_h, rhs_hi), (w_h, rhs_lo), (w_l, rhs_hi))):
                        for piece in range(3):
                            ins = pe.matmul(acc[s][:, piece, :], w[:, first_k + n, :],
                                            x[:, k, piece * NP:(piece + 1) * NP],
                                            start=(n == 0 and q == 0), stop=(n == len(ks) - 1 and q == 2))
                ins.then_inc(acc_full, 1)

            def aux_round(rnd, emit):
                pe.wait_ge(aux_free, rnd)
                emit().then_inc(aux_full, 1)

            pe.wait_ge(const_done, 1)
            for j in range(NTILE):
                rows = TILE_ROWS[j]
                pe.wait_ge(x_scaled, j + 1)
                if j >= 3:
                    pe.wait_ge(x_lo, j - 2)
                for k in range(KD):
                    b = 2 * (j % 3) + k // 4
                    ins = pe.transpose(PS[:, b, (k % 4) * P:(k % 4) * P + rows], xtok[0:rows, j, k * P:(k + 1) * P],
                                       ident[0:rows, 0:rows])
                ins.then_inc(xt_full, 1)

            def turn_consts():
                pe.wait_ge(const_in, 16 * 9)
                nch = 2 * NFF
                for a in range(4):
                    pe.transpose(aux[:, a * nch:(a + 1) * nch], cst[0:nch, a, :], ident[0:nch, 0:nch])
                pe.transpose(aux[:, 4 * nch:4 * nch + KD], cst[0:KD, 4, :], ident[0:KD, 0:KD])
                pe.transpose(aux[:, 4 * nch + KD:4 * nch + KD + NG], cst[0:NG, 5, :], ident[0:NG, 0:NG])
                pe.matmul(aux[:, 512:512 + SKEYS], rep8[0:8].rearrange("p a b -> p (a b)"), mask8[0:8, :],
                          start=True, stop=True)
                return pe.matmul(aux[:, 768:770], rep4[0:4].rearrange("p a b c -> p (a b c)"), sink_t[0:4, :],
                                 start=True, stop=True)

            def turn_conv_states():
                pe.wait_ge(convst_in, 16)
                for c in range(2 * NFF):
                    ins = pe.transpose(aux[:, c * 16:(c + 1) * 16], convst[0:16, c * P:(c + 1) * P], ident[0:16, 0:16])
                return ins

            def turn_pool_states():
                n = DEC_B * PSTATE
                for g in range(NG):
                    ins = pe.transpose(aux[:, g * P:g * P + n], pst[0:n, g * P:(g + 1) * P], ident[0:n, 0:n])
                return ins

            def turn_cached_k():
                for b in range(DEC_B):
                    ins = pe.transpose(aux[:, b * P:(b + 1) * P], ktok[:, b, :], ident[:, :])
                return ins

            def turn_u():
                pe.wait_ge(proj_done, 4)
                pe.wait_ge(u_packed, 1)
                for g in range(NG):
                    pe.transpose(aux[0:PSTATE, g * P:(g + 1) * P], uext[:, g, SEQ:SEQ + PSTATE], ident[:, :])
                for g in range(NG):
                    ins = pe.transpose(aux[0:NSAMP, 512 + g * P:512 + (g + 1) * P], upack[:, g, :], ident[:, :])
                return ins

            def turn_k():
                pe.wait_ge(proj_done, 11)
                pe.transpose(aux[:, 0:P], kT[:, SEQ:SEQ + WIN], ident[:, :])
                return pe.transpose(aux[0:NSAMP, 512:512 + P], kT[:, WIN + SEQ:WIN + T], ident[:, :])

            def turn_v():
                pe.wait_ge(proj_done, 13)
                for n in range(NBLK):
                    ins = pe.transpose(aux[:, n * P:(n + 1) * P], vT[:, n * P:(n + 1) * P], ident[:, :])
                return ins

            def turn_new_v():
                for b in range(DEC_B):
                    ins = pe.transpose(aux[0:DEC_T, b * P:(b + 1) * P],
                                       vT[:, SEQ + b * DEC_T:SEQ + (b + 1) * DEC_T], ident[:, :])
                return ins

            early = {0: {4: (AUX_CONST, turn_consts)}, 1: {4: (AUX_CONV, turn_conv_states)},
                     2: {4: (AUX_POOL, turn_pool_states)}, 3: {4: (AUX_KC, turn_cached_k)},
                     5: {4: (AUX_U, turn_u)}, 12: {4: (AUX_K, turn_k)}}
            for f, (kind, n) in enumerate(ENTRIES):
                if f >= 2:
                    pe.wait_ge(proj_done, f - 1)
                if kind == "pool":
                    pe.wait_ge(d_done, n + 1)
                    if n == 0:
                        pe.wait_ge(wgrp_in, 16)
                    for piece in range(3):
                        ins = pe.matmul(acc[f % 2][:, piece, :], wgrp[:, n, :], dT[:, piece * NP:(piece + 1) * NP],
                                        start=True, stop=True)
                    ins.then_inc(acc_full, 1)
                    continue
                c = FIRST_CHUNK[kind] + n
                if c == 0:
                    pe.wait_ge(x_lo, NTILE)
                    pe.wait_ge(const_done, 2)
                pe.wait_ge(w_lo, c + 1)
                hooks = {k: (lambda r=r, e=e: aux_round(r, e)) for k, (r, e) in early.get(f, {}).items()}
                gemm(f % 2, c, 0, range(KD), h_hi, h_lo, hooks)
            aux_round(AUX_V, turn_v)
            aux_round(AUX_VNEW, turn_new_v)

            def scores(n, kv):
                v = slice(kv * HD, (kv + 1) * HD)

                def emit():
                    pe.wait_ge(qk_staged, n + 1)
                    for c in range(NQ):
                        ins = pe.matmul(aux[:, c * 2 * WIN:(c + 1) * 2 * WIN], qblk[v, c, :], kblk[v, :],
                                        start=True, stop=True)
                    return ins
                return emit

            def turn_probs(s):
                def emit():
                    pe.wait_ge(prob_done, s + 1)
                    for b in range(2):
                        for c in range(NQ):
                            ins = pe.transpose(aux[:, (b * NQ + c) * P:(b * NQ + c + 1) * P],
                                               prob[:, c, b * WIN:(b + 1) * WIN], ident[:, :])
                    return ins
                return emit

            def values(n, kv):
                v = slice(kv * HD, (kv + 1) * HD)

                def emit():
                    pe.wait_ge(v_staged, n + 1)
                    for b in range(2):
                        ins = pe.matmul(aux[v, 0:NQ * P], vblk[:, b, v], probT[:, b, :], start=(b == 0), stop=(b == 1))
                    return ins
                return emit

            def sample_scores(h):
                def emit():
                    for kv in range(2):
                        v = slice(kv * HD, (kv + 1) * HD)
                        for i in range(4):
                            b = 4 * h + i
                            q = qpack[v, b].rearrange("p c t -> p (c t)")
                            rows = slice(32 * i, 32 * i + 32)
                            pe.matmul(aux[rows, kv * 512:kv * 512 + WIN], q, kcT[v, b, :], start=True, stop=True)
                            ins = pe.matmul(aux[rows, kv * 512 + WIN:kv * 512 + SKEYS], q,
                                            kT[v, WIN + SEQ + b * DEC_T:WIN + SEQ + (b + 1) * DEC_T],
                                            start=True, stop=True)
                    return ins
                return emit

            def sample_turn(h):
                def emit():
                    pe.wait_ge(sprob_done, h + 1)
                    for kv in range(2):
                        pe.transpose(aux[:, kv * 512:kv * 512 + P], sprob[:, kv, 0:WIN], ident[:, :])
                        ins = pe.transpose(aux[0:DEC_T, kv * 512 + P:kv * 512 + 2 * P], sprob[:, kv, WIN:SKEYS],
                                           ident[:, :])
                    return ins
                return emit

            def sample_values(h):
                def emit():
                    for kv in range(2):
                        v = slice(kv * HD, (kv + 1) * HD)
                        for i in range(4):
                            b = 4 * h + i
                            col = slice(32 * i, 32 * i + 32)
                            out = aux[v, kv * 512 + 32 * i:kv * 512 + 32 * i + 32]
                            pe.matmul(out, vc[:, b, v], sprob_c[:, kv, col], start=True, stop=False)
                            ins = pe.matmul(out, vnew[0:DEC_T, b, v], sprob_n[0:DEC_T, kv, col], start=False, stop=True)
                    return ins
                return emit

            def gate_block(n, first, last):
                for kv in range(2):
                    s = n * 2 + kv
                    c = CHUNK_GATE + kv
                    pe.wait_ge(w_lo, n * 2 + (c + 1))
                    pe.wait_ge(proj_done, n * 2 + (FILL_GATE + kv - 1))
                    hooks = {}

                    def at_k(k, rnd, emit):
                        before = hooks.get(k)

                        def run():
                            if before:
                                before()
                            aux_round(rnd, emit)
                        hooks[k] = run
                    if first:
                        r_s, r_t, r_v = AUX_SAMPLE[kv]
                        at_k(2, r_s, sample_scores(kv))
                        at_k(4, aux_turn(s), turn_probs(s))
                        at_k(5, aux_values(s), values(n, kv))
                        at_k(6, r_t, sample_turn(kv))
                        at_k(7, r_v, sample_values(kv))
                    else:
                        at_k(5, aux_turn(s), turn_probs(s))
                        at_k(6, aux_values(s), values(n, kv))
                    if kv == 0:
                        at_k(7, aux_scores(s + 1), scores(n, 1))
                    elif not last:
                        at_k(7, aux_scores(s + 1), scores(n + 1, 0))
                    gemm(kv, c, 0, range(KD), h_hi, h_lo, hooks)

            aux_round(aux_scores(0), scores(0, 0))
            gate_block(0, True, False)
            with pe.Fori(0, 6) as i:
                gate_block(i + 1, False, False)
            gate_block(7, False, True)

            def branch(m, half, ready=None):
                c = CHUNK_BRANCH + half
                pe.wait_ge(w_lo, m + (CHUNK_BRANCH + 1))
                if not ready:
                    pe.wait_ge(acc_free, m * 2 - 1)
                gemm(0, c, 0, range(0, 4), ao_hi, ao_lo, ready=ready)
                if not ready:
                    pe.wait_ge(acc_free, m * 2)
                gemm(1, c, 4, range(4, 8), ao_hi, ao_lo, ready=ready)

            pe.wait_ge(proj_done, FILL_BRANCH)
            branch(0, 0, ready=lambda k: pe.wait_ge(ao_lo_done, k + 1))
            branch(1, 1)
            with pe.Fori(0, 3) as i:
                branch(i * 2 + 2, 0)
                branch(i * 2 + 3, 1)

            def project(m, half, ready=None):
                pe.wait_ge(w_lo, m + (CHUNK_OUT + 1))
                pe.wait_ge(acc_free, m + (FILL_OUT - 1) - FILL_BRANCH)

                def turn_x():
                    pe.wait_ge(xcol_in[half], (m - half) * 16 + 32)
                    for j in range(NTILE - 2):
                        ins = pe.transpose(aux[:, j * P:(j + 1) * P], xcol[half][:, j, :], ident[:, :])
                    return ins

                def turn_x_last():
                    pe.transpose(aux[:, 0:P], xcol[half][:, NTILE - 2, :], ident[:, :])
                    return pe.transpose(aux[:, P:P + NSAMP], xcol[half][0:NSAMP, NTILE - 1, :], ident[0:NSAMP, 0:NSAMP])

                gemm(half, CHUNK_OUT + half, 0, range(KD), mx_hi, mx_lo,
                     {1: lambda: aux_round(m * 2 + AUX_X, turn_x), 5: lambda: aux_round(m * 2 + (AUX_X + 1), turn_x_last)},
                     ready)

            project(0, 0, ready=lambda k: pe.wait_ge(mix_lo_done, k + 1))
            project(1, 1)
            with pe.Fori(0, 3) as i:
                project(i * 2 + 2, 0)
                project(i * 2 + 3, 1)

            def token_sums(rnd, total, sums):
                def emit():
                    pe.wait_ge(sq_added, total)
                    for j, rows in enumerate(TILE_ROWS):
                        ins = pe.matmul(aux[0:rows, j:j + 1], sums[:, j * P:j * P + rows], ones[:, 0:1],
                                        start=True, stop=True)
                    return ins
                aux_round(rnd, emit)

            token_sums(AUX_SSQ, KD, sqsum)
            pe.wait_ge(diag_done, 1)
            for j in range(NTILE):
                n = P if j < NTILE - 1 else TP - SEQ
                ins = pe.matmul(bcast[:, j * P:j * P + n], ones[:, :], diag[:, j, 0:n], start=True, stop=True)
            ins.then_inc(bc_full, 1)

            def turn_tails(i, e, val):
                def emit():
                    pe.wait_ge(ext_done, i * 4 + (2 * e + val + 1))
                    return pe.transpose(aux[0:CSTATE + 16, 0:P], tpack[:, val, :], ident[:, :])
                return lambda: aux_round(i * 4 + (AUX_TAIL + 2 * e + val), emit)

            def up(c, s, i, add, hook, ready=None):
                pe.wait_ge(w_lo, i * 4 + (CHUNK_UP + add + 1))
                gemm(s, c, 0, range(KD), h2_hi, h2_lo, {3: hook} if hook else None, ready)

            def down(i, hooks={}, last=False):
                pe.wait_ge(dn_lo_done, i + 1)
                pe.wait_ge(act_lo_done, i * 2 + 2)
                for m in range(KD):
                    if m < 2:
                        pe.wait_ge(ext_done, i * 4 + (4 if last else 4 + m))
                    else:
                        pe.wait_ge(acc_free, i * 8 + (FILL_FFN - FILL_BRANCH + m - 1))
                    for e in range(2):
                        for q, (w, x) in enumerate(((dn_hi, act_hi), (dn_hi, act_lo), (dn_lo, act_hi))):
                            for piece in range(3):
                                ins = pe.matmul(acc[m % 2][:, piece, :], w[:, e, m * P:(m + 1) * P],
                                                x[:, e, piece * NP:(piece + 1) * NP],
                                                start=(e == 0 and q == 0), stop=(e == 1 and q == 2))
                    ins.then_inc(acc_full, 1)
                    if m in hooks:
                        hooks[m]()

            def ffn(i, last):
                base = FILL_FFN - FILL_BRANCH
                pe.wait_ge(acc_free, i * 8 + (base - 1))
                up(1, 0, i, 1, turn_tails(i, 0, 0))
                pe.wait_ge(acc_free, i * 8 + base)
                pe.wait_ge(ext_done, i * 4 + 1)
                up(0, 1, i, 2, turn_tails(i, 0, 1))
                pe.wait_ge(ext_done, i * 4 + 2)
                up(1, 0, i, 3, turn_tails(i, 1, 0))
                if not last:
                    pe.wait_ge(ext_done, i * 4 + 3)
                    up(0, 1, i, 4, turn_tails(i, 1, 1))
                    down(i)

            up(0, 1, 0, 0, None, ready=lambda k: pe.wait_ge(h2_lo_done, k + 1))
            with pe.Fori(0, NFF // 2 - 1) as i:
                ffn(i, False)
            i = NFF // 2 - 1
            ffn(i, True)

            def turn_y(m):
                def tiles():
                    pe.wait_ge(acc_free, FILL_FFN - FILL_BRANCH + 8 * i + m + 1)
                    for j in range(NTILE - 1):
                        ins = pe.transpose(aux[:, j * P:(j + 1) * P], y[:, m, j * P:(j + 1) * P], ident[:, :])
                    return ins

                def last_tile():
                    return pe.transpose(aux[0:NSAMP, 0:P], y[:, m, SEQ:T], ident[:, :])
                return lambda: (aux_round(AUX_Y + 2 * m, tiles), aux_round(AUX_Y + 2 * m + 1, last_tile))

            hooks = {m: turn_y(m - 1) for m in range(1, KD)}
            hooks[0] = turn_tails(i, 1, 1)
            down(i, hooks, True)
            turn_y(KD - 1)()
            token_sums(AUX_SSQ2, 2 * KD, sqsum2)

        def x_banks(j, rows):
            b = 2 * (j % 3)
            return PS[:, b:b + 2, :].rearrange("p b (k t) -> p (b k) t", k=4)[:, :, 0:rows]

        def copy_pieces(copy, dst, first, samp, width, s):
            copy(dst[:, first:first + 2 * NP].rearrange("p (a n) -> p a n", a=2), acc[s][:, 0:2, :])
            copy(dst[:, first + 2 * NP:first + SEQ], acc[s][:, 2, 0:SEQ - 2 * NP])
            return copy(samples(dst, samp, width),
                        acc[s][:, 2, SEQ - 2 * NP:T - 2 * NP].rearrange("p (b t) -> p b t", b=DEC_B))

        def pieces(t):
            return t.rearrange("p (a n) -> p a n", a=3)

        @block.scalar
        def _(act):
            def copy(dst, src):
                return act.activation(dst, src, ACT.Copy)

            def split_hi(half, pair):
                act.wait_ge(raw_in[half], landed(pair))
                copy(up_hi[:, half], raw[:, half]).then_inc(w_hi, 1)

            def x_split(j):
                rows = TILE_ROWS[j]
                act.wait_ge(xt_full, j + 1)
                copy(h_hi[:, :, j * P:j * P + rows], x_banks(j, rows)).then_inc(x_hi, 1)

            act.wait_ge(const_done, 1)
            for j in range(NTILE):
                rows = TILE_ROWS[j]
                act.wait_ge(x_in[j], 16)
                if j:
                    act.wait_ge(x_sq, j)
                act.activation(sq_junk[0:rows, :], xtok[0:rows, j, :], ACT.Square, accum_out=ssq[0:rows, j:j + 1])\
                    .then_inc(x_sq, 1)
                act.wait_ge(x_ms, j + 1)
                act.activation(root[0:rows, j:j + 1], ssq[0:rows, j:j + 1], ACT.Sqrt).then_inc(x_root, 1)
                if j >= 2:
                    x_split(j - 2)
                if j == 5:
                    split_hi(0, 0)
            split_hi(1, 0)
            x_split(NTILE - 2)
            x_split(NTILE - 1)

            for f, (kind, n) in enumerate(ENTRIES):
                act.wait_ge(acc_full, f + 1)
                if kind == "u":
                    ins = copy_pieces(copy, uext[:, n, :], PSTATE, USAMP, PSTATE + DEC_T, f % 2)
                elif kind == "q":
                    ins = copy(pieces(qT[:, n, :]), acc[f % 2])
                elif kind == "k":
                    ins = copy(pieces(kT[:, WIN:WIN + TP]), acc[f % 2])
                elif kind == "v":
                    ins = copy(pieces(vT[:, :]), acc[f % 2])
                else:
                    ins = act.activation(pieces(uext[:, n, 0:TP]), acc[f % 2], ACT.Copy, scale=pscale[:, n:n + 1])
                ins.then_inc(proj_done, 1)
                if kind != "pool":
                    c = FIRST_CHUNK[kind] + n + 2
                    split_hi(c % 2, c - c % 2)

            def exps(s):
                act.wait_ge(smax_done, s + 1)
                for c in range(NQ):
                    act.activation(prob[:, c, :], prob[:, c, :], ACT.Exp, bias=snegm[:, c:c + 1],
                                   accum_out=ssum[:, c:c + 1])
                act.activation(sesink[:, :], sesink[:, :], ACT.Exp).then_inc(exp_done, 1)

            def sample_exps(h):
                act.wait_ge(ssmax_done, h + 1)
                for kv in range(2):
                    act.activation(sprob[:, kv, :], sprob[:, kv, :], ACT.Exp, bias=snegm[:, kv:kv + 1],
                                   accum_out=ssum[:, kv:kv + 1])
                act.activation(sesink[:, 0:2], sesink[:, 0:2], ACT.Exp).then_inc(sexp_done, 1)

            def gate_block(n, first, last):
                for kv in range(2):
                    if first:
                        sample_exps(kv)
                    if not (last and kv):
                        exps(n * 2 + (kv + 1))
                    act.wait_ge(acc_full, n * 2 + (FILL_GATE + kv + 1))
                    if not first:
                        act.wait_ge(gate_out[kv], n * 16)
                    act.activation(pieces(gate_st[:, kv, :]), acc[kv], ACT.Sigmoid).then_inc(proj_done, 1)
                    split_hi(kv, n * 2 + (CHUNK_GATE + 2))

            exps(0)
            gate_block(0, True, False)
            with act.Fori(0, 6) as i:
                gate_block(i + 1, False, False)
            gate_block(7, False, True)

            for k in range(KD):
                if k == 4:
                    act.wait_ge(aux_free, AUX_X)
                if k == 0:
                    act.wait_ge(proj_done, FILL_GATE)
                copy(ao_hi[:, k, :], uext[:, k, 0:TP] if k < 4 else qT[:, k - 4, :]).then_inc(ao_hi_done, 1)

            def mix(m, half):
                act.wait_ge(mix_sum, m + 1)
                copy(mx_hi[:, bass.ds(m, 1), :], gates[:, half, 0:1, :]).then_inc(mix_hi_done, 1)
                split_hi(half, (m - half) + (CHUNK_BRANCH + 2))

            with act.Fori(0, 4) as i:
                for half in range(2):
                    mix(i * 2 + half, half)

            act.wait_ge(pads_done, 1)

            def project(m, half):
                act.wait_ge(aux_full, m * 2 + (AUX_X + 1))
                act.wait_ge(acc_free, m + (FILL_OUT - FILL_BRANCH - 1))
                copy(xT[:, half, 0:SEQ - P], aux[:, 0:SEQ - P]).then_inc(aux_free, 1)
                act.wait_ge(aux_full, m * 2 + (AUX_X + 2))
                copy(xT[:, half, SEQ - P:T], aux[:, 0:P + NSAMP]).then_inc(aux_free, 1)
                act.wait_ge(acc_free, m + (FILL_OUT - FILL_BRANCH + 1))
                act.wait_ge(sq_added, m)
                act.activation(sq[:, :].unsqueeze(1), y[:, bass.ds(m, 1), :], ACT.Square).then_inc(sq_done, 1)
                split_hi(half, (m - half) + (CHUNK_OUT + 2))

            with act.Fori(0, 4) as i:
                for half in range(2):
                    project(i * 2 + half, half)

            act.wait_ge(aux_free, AUX_SSQ + 1)
            act.activation(root[:, :], ssq[:, :], ACT.Sqrt).then_inc(root2, 1)
            for k in range(KD):
                act.wait_ge(h2_sum, k + 1)
                copy(h2_hi[:, k, :], xT[:, k % 2, :]).then_inc(h2_hi_done, 1)

            def copy_up(s, fill, val, u, ch):
                act.wait_ge(acc_full, fill)
                act.wait_ge(conv_done, u)
                ext = ext_val if val else ext_gate
                last = acc[s][:, 2, SEQ - 2 * NP:T - 2 * NP].rearrange("p (b t) -> p b t", b=DEC_B)
                copy(tpack[:, val, 0:CSTATE], acc[s][:, 2, SEQ - CSTATE - 2 * NP:SEQ - 2 * NP])
                copy(tpack[:, val, CSTATE:].rearrange("p (b w) -> p b w", b=DEC_B), last[:, :, DEC_T - CSTATE:DEC_T])
                copy(ext[:, ESAMP:EXT].rearrange("p (b w) -> p b w", b=DEC_B)[:, :, 0:CSTATE],
                     cstate[:, bass.ds(ch, 1), :].rearrange("p o (b w) -> p (o b) w", b=DEC_B))
                copy_pieces(copy, ext, CSTATE, ESAMP, CSTATE + DEC_T, s).then_inc(ext_done, 1)

            def silu(j, u1):
                act.wait_ge(conv_done, u1)
                act.activation(conv_gate[:, 0:NCONV], conv_gate[:, 0:NCONV], ACT.Silu).then_inc(silu_done, 1)

            def act_split(j, e):
                act.wait_ge(prod_done, j + 1)
                act.wait_ge(pads_done, 2)
                copy(act_hi[:, e, 0:SEQ], conv_val[:, 0:SEQ])
                copy(act_hi[:, e, SEQ:T].rearrange("p (b t) -> p b t", b=DEC_B),
                     samples(conv_val, ESAMP - CSTATE, CSTATE + DEC_T)).then_inc(act_hi_done, 1)

            def tails(i, e, val):
                act.wait_ge(aux_full, i * 4 + (AUX_TAIL + 2 * e + val + 1))
                copy(tail_rows[0:CSTATE + 16, val, e, :], aux[0:CSTATE + 16, 0:P]).then_inc(aux_free, 1)

            copy_up(1, FILL_FFN + 1, 0, 0, 0)
            split_hi(0, CHUNK_UP + 2)
            silu(0, 1)

            def ffn(i, last):
                fill = i * 12 + FILL_FFN
                act.wait_ge(tail_out, i * 64)
                tails(i, 0, 0)
                copy_up(0, fill + 2, 1, i * 4, i * 2 + NFF)
                split_hi(1, i * 4 + (CHUNK_UP + 2))
                act.wait_ge(dn_in, i * 16 + 16)
                copy(dn_hi[:, :, :], raw_dn[:, :, :]).then_inc(dn_hi_done, 1)
                act_split(i * 2, 0)
                tails(i, 0, 1)
                copy_up(1, fill + 3, 0, i * 4 + 1, i * 2 + 1)
                if not last:
                    split_hi(0, i * 4 + (CHUNK_UP + 4))
                silu(i * 2 + 1, i * 4 + 3)
                tails(i, 1, 0)
                copy_up(0, fill + 4, 1, i * 4 + 2, i * 2 + (NFF + 1))
                if not last:
                    split_hi(1, i * 4 + (CHUNK_UP + 4))
                act_split(i * 2 + 1, 1)
                if not last:
                    tails(i, 1, 1)
                    copy_up(1, fill + 5, 0, i * 4 + 3, i * 2 + 2)
                    split_hi(0, i * 4 + (CHUNK_UP + 6))
                    silu(i * 2 + 2, i * 4 + 5)

            with act.Fori(0, NFF // 2 - 1) as i:
                ffn(i, False)
            i = NFF // 2 - 1
            ffn(i, True)
            tails(i, 1, 1)
            for m in range(KD):
                act.wait_ge(acc_free, FILL_FFN - FILL_BRANCH + 8 * i + m + 1)
                act.wait_ge(sq_added, KD + m)
                act.activation(sq2[:, :], y[:, m, :], ACT.Square).then_inc(sq_done, 1)
                act.wait_ge(aux_full, AUX_Y + 2 * m + 1)
                copy(ytok[:, 0:NTILE - 1, m * P:(m + 1) * P], aux[:, :].rearrange("p (j f) -> p j f", f=P))\
                    .then_inc(aux_free, 1)
                act.wait_ge(aux_full, AUX_Y + 2 * m + 2)
                copy(ytok[0:NSAMP, NTILE - 1, m * P:(m + 1) * P], aux[0:NSAMP, 0:P]).then_inc(aux_free, 1)
            act.wait_ge(aux_free, AUX_SSQ2 + 1)
            act.activation(root[:, :], ssq[:, :], ACT.Sqrt).then_inc(root2, 1)

        @block.vector
        def _(dve):
            chain = Chain(dve, dve_step)
            link = chain.link

            def split_lo(half, c1):
                dve.wait_ge(w_hi, c1)
                dve.tensor_tensor(up_lo[:, half], raw[:, half], up_hi[:, half].bitcast(F32), ALU.subtract)\
                    .then_inc(w_lo, 1)

            def x_split(j):
                rows = TILE_ROWS[j]
                dve.wait_ge(x_hi, j + 1)
                col = slice(j * P, j * P + rows)
                dve.tensor_tensor(h_lo[:, :, col], x_banks(j, rows), h_hi[:, :, col].bitcast(F32), ALU.subtract)\
                    .then_inc(x_lo, 1)

            for j in range(NTILE):
                rows = TILE_ROWS[j]
                dve.wait_ge(x_sq, j + 1)
                dve.tensor_scalar(ssq[0:rows, j:j + 1], ssq[0:rows, j:j + 1], 1.0 / D, EPS, ALU.mult, ALU.add)\
                    .then_inc(x_ms, 1)
                dve.wait_ge(x_root, j + 1)
                link(dve.reciprocal(rstd[0:rows, j:j + 1], root[0:rows, j:j + 1]))
                if j == 0:
                    dve.wait_ge(gmix_in, 16)
                dve.scalar_tensor_tensor(xtok[0:rows, j, :], xtok[0:rows, j, :], rstd[0:rows, j:j + 1],
                                         gmix_b[0:rows, :], ALU.mult, ALU.mult).then_inc(x_scaled, 1)
                if j >= 2:
                    x_split(j - 2)
                if j == 6:
                    split_lo(0, 1)
            split_lo(1, 2)
            x_split(NTILE - 2)
            x_split(NTILE - 1)

            def take(rnd):
                dve.wait_ge(aux_full, rnd + 1)

            def pool_group(g):
                w = 2 << g
                u = uext[:, g, :]
                dve.wait_ge(proj_done, g + 1)
                dve.wait_ge(d_done, g)
                src = u
                for level in range(g + 1):
                    dst = (sum_a, sum_b)[level % 2]
                    lo, step = (2 << level) - 1, 1 << level
                    link(dve.tensor_tensor(dst[:, lo:UEXT], src[:, lo:UEXT], src[:, lo - step:UEXT - step], ALU.add))
                    src = dst
                if g:
                    dve.wait_ge(acc_full, ENTRIES.index(("pool", g - 1)) + 1)
                link(dve.scalar_tensor_tensor(dT[:, 0:SEQ], src[:, PSTATE:PSTATE + SEQ], 1.0 / w,
                                              u[:, PSTATE:PSTATE + SEQ], ALU.mult, ALU.subtract))
                link(dve.tensor_tensor(dT[:, 0:w - 1], src[:, PSTATE:PSTATE + w - 1], rcount[:, 0:w - 1], ALU.mult))
                link(dve.tensor_tensor(dT[:, 0:w - 1], dT[:, 0:w - 1], u[:, PSTATE:PSTATE + w - 1], ALU.subtract))
                dve.scalar_tensor_tensor(dT[:, SEQ:T].rearrange("p (b t) -> p b t", b=DEC_B),
                                         samples(src, USAMP, PSTATE + DEC_T), 1.0 / w,
                                         samples(u, USAMP, PSTATE + DEC_T), ALU.mult, ALU.subtract).then_inc(d_done, 1)

            for f, (kind, n) in enumerate(ENTRIES):
                if f == 0:
                    take(AUX_CONST)
                    dve.tensor_copy(cols[:, :], aux[:, 0:8 * NFF + KD + NG])
                    dve.tensor_copy(smask[:, :], aux[:, 512:512 + SKEYS])
                    dve.tensor_copy(sink_s[:, :], aux[:, 768:770]).then_inc(aux_free, 1)
                elif f == 1:
                    take(AUX_CONV)
                    dve.tensor_copy(cstate[:, :, :], aux[:, 0:2 * NFF * 16].rearrange("p (c s) -> p c s", s=16))\
                        .then_inc(aux_free, 1)
                elif f == 2:
                    take(AUX_POOL)
                    for g in range(NG):
                        dst = uext[:, g, USAMP:UEXT].rearrange("p (b w) -> p b w", b=DEC_B)[:, :, 0:PSTATE]
                        src = aux[:, g * P:g * P + DEC_B * PSTATE].rearrange("p (b w) -> p b w", b=DEC_B)
                        ins = dve.tensor_copy(dst, src)
                    ins.then_inc(aux_free, 1)
                elif f == 3:
                    take(AUX_KC)
                    dve.tensor_copy(kcT[:, :, :], aux[:, :].rearrange("p (b t) -> p b t", b=DEC_B)).then_inc(aux_free, 1)
                elif f == 4:
                    dve.wait_ge(uzero_done, 1)
                    dve.wait_ge(aux_free, AUX_POOL + 1)
                    link(dve.memset(dT[:, PADS], 0.0))
                    pool_group(0)
                elif f == 5:
                    take(AUX_U)
                    dve.tensor_copy(uout_p[0:PSTATE, :], aux[0:PSTATE, 0:POOL_W])
                    dve.tensor_copy(uout_s[0:NSAMP, :], aux[0:NSAMP, 512:1024]).then_inc(aux_free, 1)
                elif f == 12:
                    take(AUX_K)
                    dve.tensor_copy(kout_p[:, :], aux[:, 0:P])
                    dve.tensor_copy(kout_s[0:NSAMP, :], aux[0:NSAMP, 512:512 + P]).then_inc(aux_free, 1)
                if kind == "pool":
                    if n + 1 < NG:
                        pool_group(n + 1)
                else:
                    c = FIRST_CHUNK[kind] + n + 2
                    split_lo(c % 2, c + 1)
            take(AUX_V)
            dve.tensor_copy(vtok[:, 1:1 + NBLK, :], aux[:, :].rearrange("p (n d) -> p n d", n=NBLK)).then_inc(aux_free, 1)
            take(AUX_VNEW)
            dve.tensor_copy(vnew[0:DEC_T, :, :], aux[0:DEC_T, :].rearrange("p (b d) -> p b d", b=DEC_B))\
                .then_inc(aux_free, 1)

            def score_max(rnd, scores, msk, out, sink, g, done):
                dve.wait_ge(aux_full, rnd + 1)
                n = out.shape[-1]
                dve.scalar_tensor_tensor(out, scores, SCALE, msk.unsqueeze(1).to_broadcast([P, g, n]), ALU.mult, ALU.add)\
                    .then_inc(aux_free, 1)
                dve.wait_ge(aux_free, rnd + 1)
                link(dve.tensor_reduce(smx[:, 0:g], out, AX.X, ALU.max))
                link(dve.tensor_tensor(smx[:, 0:g], smx[:, 0:g], sink, ALU.max))
                link(dve.tensor_scalar(snegm[:, 0:g], smx[:, 0:g], -1.0, None, ALU.mult))
                dve.tensor_tensor(sesink[:, 0:g], sink, snegm[:, 0:g], ALU.add).then_inc(done, 1)

            def normalise(out, g, done):
                link(dve.tensor_tensor(sden[:, 0:g], ssum[:, 0:g], sesink[:, 0:g], ALU.add))
                link(dve.reciprocal(srec[:, 0:g], sden[:, 0:g]))
                dve.tensor_tensor(out, out, srec[:, 0:g].unsqueeze(2).to_broadcast([P, g, out.shape[-1]]), ALU.mult)\
                    .then_inc(done, 1)

            def softmax(s, kv, msk):
                score_max(aux_scores(s), aux[:, :].rearrange("p (c n) -> p c n", c=NQ), msk, prob[:, :, :],
                          sink_b[:, kv * NQ:(kv + 1) * NQ], NQ, smax_done)
                dve.wait_ge(exp_done, s + 1)
                normalise(prob[:, :, :], NQ, prob_done)

            def take_values(n, kv):
                v = slice(kv * HD, (kv + 1) * HD)
                dve.wait_ge(aux_full, aux_values(n * 2 + kv) + 1)
                dve.tensor_copy(qT[v, :, bass.ds(n * WIN, WIN)], aux[v, 0:NQ * P].rearrange("p (c t) -> p c t", c=NQ))\
                    .then_inc(aux_free, 1)

            def take_probs(s):
                dve.wait_ge(aux_full, aux_turn(s) + 1)
                dve.tensor_copy(probT[:, :, :], aux[:, :].rearrange("p (b n) -> p b n", b=2)).then_inc(aux_free, 1)

            def sample_part(h):
                r_s, r_t, r_v = AUX_SAMPLE[h]
                banks = aux[:, :].rearrange("p (v n) -> p v n", v=2)
                score_max(r_s, banks[:, :, 0:SKEYS], smask[:, :], sprob[:, :, :], sink_s[:, :], 2, ssmax_done)
                take_probs(h)
                take_values(0, h)
                dve.wait_ge(sexp_done, h + 1)
                normalise(sprob[:, :, :], 2, sprob_done)
                take(r_t)
                dve.tensor_copy(sprob_c[:, :, :], banks[:, :, 0:P])
                dve.tensor_copy(sprob_n[0:DEC_T, :, :], banks[0:DEC_T, :, P:2 * P]).then_inc(aux_free, 1)
                take(r_v)
                for kv in range(2):
                    v = slice(kv * HD, (kv + 1) * HD)
                    for i in range(4):
                        col = SEQ + (4 * h + i) * DEC_T
                        ins = dve.tensor_copy(qT[v, :, col:col + DEC_T],
                                              banks[v, kv, 32 * i:32 * i + 32].rearrange("p (c t) -> p c t", c=NQ))
                ins.then_inc(aux_free, 1)

            def gate_block(n, first, last):
                for kv in range(2):
                    if first:
                        sample_part(kv)
                    else:
                        take_probs(n * 2 + kv)
                        take_values(n, kv)
                    if not (last and kv):
                        softmax(n * 2 + (kv + 1), (kv + 1) % 2, (mask_first if first and kv == 0 else mask)[:, :])
                    split_lo(kv, n * 2 + (CHUNK_GATE + kv + 3))

            dve.wait_ge(u_out, 16 * 9)
            dve.wait_ge(kv_out, 16 * 11)
            softmax(0, 0, mask_first[:, :])
            gate_block(0, True, False)
            with dve.Fori(0, 6) as i:
                chain.enter(i, 10)
                gate_block(i + 1, False, False)
            chain.leave(6, 10)
            gate_block(7, False, True)

            for k in range(KD):
                dve.wait_ge(ao_hi_done, k + 1)
                dve.tensor_tensor(ao_lo[:, k, :], uext[:, k, 0:TP] if k < 4 else qT[:, k - 4, :],
                                  ao_hi[:, k, :].bitcast(F32), ALU.subtract).then_inc(ao_lo_done, 1)

            def mix(m, half):
                dve.wait_ge(gate_in[half], (m - half) * 16 + 32)
                for b in range(2):
                    dve.wait_ge(acc_full, m * 2 + (FILL_BRANCH + b + 1))
                    g = pieces(gates[:, half, b, :])
                    dve.tensor_tensor(g, acc[b], g, ALU.mult).then_inc(acc_free, 1)
                dve.wait_ge(acc_free, m * 2 + 2)
                dve.tensor_tensor(gates[:, half, 0, :], gates[:, half, 0, :], gates[:, half, 1, :], ALU.add)\
                    .then_inc(mix_sum, 1)
                split_lo(half, m + (CHUNK_BRANCH + 3))
                dve.wait_ge(mix_hi_done, m + 1)
                dve.tensor_tensor(mx_lo[:, bass.ds(m, 1), :], gates[:, half, 0:1, :],
                                  mx_hi[:, bass.ds(m, 1), :].bitcast(F32), ALU.subtract).then_inc(mix_lo_done, 1)

            with dve.Fori(0, 4) as i:
                for half in range(2):
                    mix(i * 2 + half, half)

            def project(m, half):
                dve.wait_ge(aux_free, m * 2 + (AUX_X + 2))
                dve.wait_ge(acc_full, m + (FILL_OUT + 1))
                dve.tensor_tensor(y[:, bass.ds(m, 1), :].rearrange("p o (a n) -> p (o a) n", a=3), acc[half],
                                  pieces(xT[:, half, :]), ALU.add).then_inc(acc_free, 1)
                split_lo(half, m + (CHUNK_OUT + 3))

            with dve.Fori(0, 4) as i:
                for half in range(2):
                    project(i * 2 + half, half)

            def mean_squares(rnd):
                take(rnd)
                dve.tensor_scalar(ssq[:, 0:NTILE - 1], aux[:, 0:NTILE - 1], 1.0 / D, EPS, ALU.mult, ALU.add)
                dve.tensor_scalar(ssq[0:NSAMP, NTILE - 1:NTILE], aux[0:NSAMP, NTILE - 1:NTILE], 1.0 / D, EPS,
                                  ALU.mult, ALU.add).then_inc(aux_free, 1)

            mean_squares(AUX_SSQ)
            dve.wait_ge(root2, 1)
            link(dve.reciprocal(rstd[:, :], root[:, :]))
            for j in range(NTILE):
                ins = dve.tensor_scalar(diag[:, j, :], ident[:, :], rstd[:, j:j + 1], None, ALU.mult)
            ins.then_inc(diag_done, 1)
            dve.wait_ge(bc_full, 1)

            def h2_low(k):
                dve.wait_ge(h2_hi_done, k + 1)
                dve.tensor_tensor(h2_lo[:, k, :], xT[:, k % 2, :], h2_hi[:, k, :].bitcast(F32), ALU.subtract)\
                    .then_inc(h2_lo_done, 1)

            for k in range(KD):
                if k >= 2:
                    dve.wait_ge(h2_lo_done, k - 1)
                dve.scalar_tensor_tensor(xT[:, k % 2, :], y[:, k, :], gffn[:, k:k + 1], bcast, ALU.mult, ALU.mult)\
                    .then_inc(h2_sum, 1)
                if k:
                    h2_low(k - 1)
            h2_low(KD - 1)

            def conv(u1, ch, val):
                ext, dst = (ext_val, conv_val) if val else (ext_gate, conv_gate)

                def tap(a):
                    return cw[:, a, bass.ds(ch, 1)]
                dve.wait_ge(ext_done, u1)
                link(dve.tensor_scalar(dst[:, 0:NCONV], ext[:, 2:EXT], tap(2), tap(3), ALU.mult, ALU.add))
                link(dve.scalar_tensor_tensor(dst[:, 0:NCONV], ext[:, 1:EXT - 1], tap(1), dst[:, 0:NCONV],
                                              ALU.mult, ALU.add))
                dve.scalar_tensor_tensor(dst[:, 0:NCONV], ext[:, 0:NCONV], tap(0), dst[:, 0:NCONV],
                                         ALU.mult, ALU.add).then_inc(conv_done, 1)

            def product(j, u1):
                dve.wait_ge(silu_done, j + 1)
                dve.wait_ge(conv_done, u1)
                dve.tensor_tensor(conv_val[:, 0:NCONV], conv_val[:, 0:NCONV], conv_gate[:, 0:NCONV], ALU.mult)\
                    .then_inc(prod_done, 1)

            def act_low(j, e):
                dve.wait_ge(act_hi_done, j + 1)
                dve.tensor_tensor(act_lo[:, e, 0:SEQ], conv_val[:, 0:SEQ], act_hi[:, e, 0:SEQ].bitcast(F32), ALU.subtract)
                dve.tensor_tensor(act_lo[:, e, SEQ:T].rearrange("p (b t) -> p b t", b=DEC_B),
                                  samples(conv_val, ESAMP - CSTATE, CSTATE + DEC_T),
                                  act_hi[:, e, SEQ:T].bitcast(F32).rearrange("p (b t) -> p b t", b=DEC_B),
                                  ALU.subtract).then_inc(act_lo_done, 1)

            conv(1, 0, 0)
            split_lo(0, CHUNK_UP + 3)

            def ffn(i, last):
                conv(i * 4 + 2, i * 2 + NFF, 1)
                product(i * 2, i * 4 + 2)
                split_lo(1, i * 4 + (CHUNK_UP + 4))
                dve.wait_ge(dn_hi_done, i + 1)
                dve.tensor_tensor(dn_lo[:, :, :], raw_dn[:, :, :], dn_hi[:, :, :].bitcast(F32), ALU.subtract)\
                    .then_inc(dn_lo_done, 1)
                act_low(i * 2, 0)
                conv(i * 4 + 3, i * 2 + 1, 0)
                if not last:
                    split_lo(0, i * 4 + (CHUNK_UP + 5))
                conv(i * 4 + 4, i * 2 + (NFF + 1), 1)
                product(i * 2 + 1, i * 4 + 4)
                if not last:
                    split_lo(1, i * 4 + (CHUNK_UP + 6))
                act_low(i * 2 + 1, 1)
                if not last:
                    conv(i * 4 + 5, i * 2 + 2, 0)
                    split_lo(0, i * 4 + (CHUNK_UP + 7))
                for m in range(KD):
                    dve.wait_ge(acc_free, i * 8 + (FILL_FFN - FILL_BRANCH + m - 7))
                    dve.wait_ge(acc_full, i * 12 + (FILL_FFN + (5 if last else 6) + m))
                    dve.tensor_tensor(pieces(y[:, m, :]), acc[m % 2], pieces(y[:, m, :]), ALU.add).then_inc(acc_free, 1)

            with dve.Fori(0, NFF // 2 - 1) as i:
                chain.enter(i, 8)
                ffn(i, False)
            chain.leave(NFF // 2 - 1, 8)
            ffn(NFF // 2 - 1, True)

            mean_squares(AUX_SSQ2)
            dve.wait_ge(root2, 2)
            link(dve.reciprocal(rstd[:, :], root[:, :]))
            dve.wait_ge(gfin_in, 16)
            dve.wait_ge(aux_free, AUX_SSQ2)
            for j, rows in enumerate(TILE_ROWS):
                dve.scalar_tensor_tensor(ytok[0:rows, j, :], ytok[0:rows, j, :], rstd[0:rows, j:j + 1],
                                         gfin_b[0:rows, :], ALU.mult, ALU.mult).then_inc(y_scaled, 1)

        @block.gpsimd
        def _(pool):
            chain = Chain(pool, pool_step)
            link = chain.link

            def select(t, compare, fill, base, pattern, mult):
                return pool.affine_select(out=t, in_=t, compare_op=compare, fill=fill, base=base, pattern=pattern,
                                          channel_multiplier=mult)

            pool.memset(ident[:, :], 0.0)
            pool.memset(ssq[:, :], 1.0)
            link(pool.memset(ones[:, :], 1.0))
            select(ident[:, :], ALU.not_equal, 1.0, 0, [[-1, P]], 1).then_inc(const_done, 1)

            for t in (h_hi, h_lo):
                pool.memset(t[:, :, PADS].bitcast(F32), 0.0)
            pool.memset(kT[:, 0:WIN], 0.0)
            pool.memset(rep8[0:8, :, :], 0.0)
            pool.memset(rep4[0:4, :, :, :], 0.0)
            pool.memset(mask8[0:8, :], 0.0)
            pool.memset(mask[:, :], 0.0)
            for t in range(PSTATE):
                pool.memset(rcount[:, t:t + 1], 1.0 / (t + 1))
            link(pool.memset(mask_first[:, 0:WIN], MASKED))
            select(rep8[0:8], ALU.not_equal, 1.0, 0, [[0, 16], [1, 8]], -1)
            select(rep4[0:4], ALU.not_equal, 1.0, 0, [[0, 4], [1, 4], [0, 8]], -1)
            link(select(mask8[0:8, :], ALU.is_ge, MASKED, 0, [[1, SKEYS]], -1))
            select(mask8[0:8, :], ALU.is_ge, MASKED, WIN, [[-1, SKEYS]], 1)
            link(select(mask[:, :], ALU.is_ge, MASKED, 0, [[1, 2 * WIN]], -1))
            link(select(mask[:, :], ALU.is_ge, MASKED, WIN, [[-1, 2 * WIN]], 1))
            pool.tensor_copy(mask_first[:, WIN:2 * WIN], mask[:, WIN:2 * WIN]).then_inc(const_done, 1)
            pool.wait_ge(xt_full, NTILE)
            pool.memset(uext[:, :, 0:PSTATE], 0.0).then_inc(uzero_done, 1)
            pool.wait_ge(aux_full, AUX_CONST + 1)
            link(pool.memset(vtok[:, 0, :], 0.0))
            pool.wait_ge(proj_done, 4)
            for g in range(NG):
                ins = pool.tensor_copy(upack[:, g, :].rearrange("p (b t) -> p b t", b=DEC_B),
                                       samples(uext[:, g, :], USAMP, PSTATE + DEC_T))
            ins.then_inc(u_packed, 1)

            def stage_qk(n, rnd):
                if rnd is not None:
                    pool.wait_ge(aux_full, rnd + 1)
                    pool.wait_ge(uzero_done, 1)
                pool.tensor_copy(qblk[:, :, :], qT[:, :, bass.ds(n * WIN, WIN)])
                pool.tensor_copy(kblk[:, :], kT[:, bass.ds(n * WIN, 2 * WIN)]).then_inc(qk_staged, 1)

            def stage_v(n, rnd):
                if rnd is not None:
                    pool.wait_ge(aux_full, rnd + 1)
                    pool.wait_ge(const_done, 2)
                pool.tensor_copy(vblk[:, :, :], vtok[:, bass.ds(n, 2), :]).then_inc(v_staged, 1)

            pool.wait_ge(proj_done, 11)
            for b in range(DEC_B):
                pool.tensor_copy(qpack[:, b, :, :], qT[:, :, SEQ + b * DEC_T:SEQ + (b + 1) * DEC_T])
            stage_qk(0, None)
            pool.wait_ge(aux_free, AUX_V + 1)
            stage_v(0, None)
            stage_qk(1, aux_scores(1))
            stage_v(1, aux_values(1))
            with pool.Fori(0, 6) as i:
                stage_qk(i + 2, aux_scores(i * 2 + 3))
                stage_v(i + 2, aux_values(i * 2 + 3))

            pool.wait_ge(acc_full, FILL_OUT)
            pool.memset(ext_gate[:, 0:CSTATE], 0.0)
            pool.memset(ext_val[:, 0:CSTATE], 0.0)
            pool.memset(xT[:, :, PADS], 0.0)
            pool.memset(sqsum[:, :], 0.0).then_inc(pads_done, 1)
            pool.wait_ge(pads_done, 1)

            def add_squares(m, total, square):
                pool.wait_ge(sq_added, m)
                pool.wait_ge(sq_done, m + 1)
                pool.tensor_tensor(total[:, :], total[:, :], square[:, :], ALU.add).then_inc(sq_added, 1)

            with pool.Fori(0, KD) as m:
                add_squares(m, sqsum, sq)

            pool.wait_ge(h2_lo_done, KD)
            for t in (act_hi, act_lo):
                ins = pool.memset(t[:, :, PADS].bitcast(F32), 0.0)
            ins.then_inc(pads_done, 1)

            i = NFF // 2 - 1
            pool.wait_ge(acc_full, FILL_FFN + 12 * i + 4)
            link(pool.memset(sqsum2[:, :], 0.0))
            for m in range(KD):
                add_squares(KD + m, sqsum2, sq2)


_INS = ["x_prompt", "x_sample", "state_pool", "cache_k", "cache_v", "state_conv", "g_mix", "w_in", "w_pool_grp",
        "pool_scale", "sinks", "w_branch_pool", "w_branch_attn", "w_out", "g_ffn", "w_up", "conv_w", "conv_b",
        "w_down", "g_final"]
_OUTS = [(1, SEQ, D), (DEC_B, DEC_T, D), (1, 1, PSTATE, POOL_W), (1, 1, WIN, 2, HD), (1, 1, WIN, 2, HD),
         (1, 1, CSTATE, 2 * D_FF), (1, DEC_B, PSTATE, POOL_W), (1, DEC_B, WIN, 2, HD), (1, DEC_B, WIN, 2, HD),
         (1, DEC_B, CSTATE, 2 * D_FF)]


def kernel(**inputs):
    import numpy as _np
    import concourse.bacc as _bacc
    from concourse import mybir as _mybir
    from concourse.bass_utils import run_bass_kernel_spmd as _run

    nc = _bacc.Bacc("TRN2", target_bir_lowering=False, num_devices=1)
    arrays, args = {}, []
    for name in _INS:
        a = _np.ascontiguousarray(inputs[name])
        arrays[f"in_{name}_dram"] = a
        args.append(nc.dram_tensor(f"in_{name}_dram", a.shape, _mybir.dt.from_np(a.dtype), kind="ExternalInput").ap())
    for i, shape in enumerate(_OUTS):
        args.append(nc.dram_tensor(f"out_{i}_dram", shape, _mybir.dt.float32, kind="ExternalOutput").ap())
    hybrid_layer(nc, *args)
    r = _run(nc, [arrays], core_ids=[0])
    return tuple(r.results[0][f"out_{i}_dram"] for i in range(len(_OUTS)))
```

```python
from contextlib import ExitStack

import concourse.bass as bass
from concourse import mybir

F32 = mybir.dt.float32
F32R = mybir.dt.float32r
ALU = mybir.AluOpType
ACT = mybir.ActivationFunctionType
AX = mybir.AxisListType

P = 128
D = 1024
SEQ = 1024
DEC_B, DEC_T = 8, 8
NSAMP = DEC_B * DEC_T
T = SEQ + NSAMP
NP = 364
TP = 3 * NP
KD = D // P
PADS = slice(T, TP)

POOL_W = D // 2
NG = 4
PSTATE = 15
UEXT = PSTATE + SEQ + DEC_B * (PSTATE + DEC_T)
USAMP = PSTATE + SEQ

HD = 64
NQ = 4
WIN = 128
NBLK = SEQ // WIN
SCALE = HD ** -0.5
MASKED = -1e30
SKEYS = WIN + DEC_T

D_FF = 2816
NFF = D_FF // P
CSTATE = 2
ESAMP = CSTATE + SEQ
EXT = ESAMP + DEC_B * (CSTATE + DEC_T)
NCONV = EXT - 2
EPS = 1e-6

NTILE = 9
TILE_ROWS = [P] * (SEQ // P) + [NSAMP]
X_GROUPS = [(0, 1), (1, 3), (3, 6), (6, NTILE)]
X_BANK = 2

N_U, N_Q = 4, 4
CHUNK_V, CHUNK_K, CHUNK_GATE = 8, 9, 10
CHUNK_BRANCH = CHUNK_GATE + 16
CHUNK_OUT = CHUNK_BRANCH + KD
CHUNK_UP = CHUNK_OUT + KD
N_CHUNKS = CHUNK_UP + 2 * NFF

ENTRIES = ([("u", g) for g in range(4)] + [("q", 0), ("q", 1), ("pool", 0), ("q", 2), ("pool", 1), ("q", 3),
           ("v", 0), ("pool", 2), ("k", 0), ("pool", 3)])
FIRST_CHUNK = {"u": 0, "q": N_U, "v": CHUNK_V, "k": CHUNK_K}
FILL_GATE = len(ENTRIES)
FILL_BRANCH = FILL_GATE + 16
FILL_OUT = FILL_BRANCH + 2 * KD
FILL_FFN = FILL_OUT + KD

AUX_CONST, AUX_CONV, AUX_POOL, AUX_KC, AUX_U, AUX_V, AUX_VNEW, AUX_K = range(8)
AUX_S0 = 8


def aux_scores(s):
    return {0: 8, 1: 14, 2: 20}[s] if isinstance(s, int) and s < 3 else s * 3 + 14


def aux_turn(s):
    return {0: 10, 1: 16}[s] if isinstance(s, int) and s < 2 else s * 3 + 15


def aux_values(s):
    return {0: 11, 1: 17}[s] if isinstance(s, int) and s < 2 else s * 3 + 16


AUX_SAMPLE = [(9, 12, 13), (15, 18, 19)]
AUX_X = 3 * 15 + 17
AUX_SSQ = AUX_X + 2 * KD
AUX_RMS = AUX_SSQ + 1
AUX_TAIL = AUX_RMS + 2
AUX_Y = AUX_TAIL + 2 * NFF

THIRDS = [(0, NP), (NP, NP), (2 * NP, T - 2 * NP)]
SEG = 3 * P
SEGS = [(0, SEG), (SEG, SEG), (2 * SEG, T - 2 * SEG)]


def landed(pair):
    return pair * 24 + 48


class Chain:

    def __init__(self, eng, sem):
        self.eng, self.sem, self.n = eng, sem, 0

    def link(self, ins):
        ins.then_inc(self.sem, 1)
        self.n = self.n + 1
        self.eng.wait_ge(self.sem, self.n)

    def enter(self, i, per):
        self.start, self.n, self.local = self.n, i * per + self.n, self.n

    def leave(self, times, per):
        self.n = self.start + times * per


def hybrid_layer(nc, x_prompt, x_sample, state_pool, cache_k, cache_v, state_conv, g_mix, w_in, w_pool_grp,
                 pool_scale, sinks, w_branch_pool, w_branch_attn, w_out, g_ffn, w_up, conv_w, conv_b, w_down,
                 g_final, y_prompt, y_sample, pool_prompt, k_prompt, v_prompt, conv_prompt,
                 pool_sample, k_sample, v_sample, conv_sample):
    x_p = x_prompt[0]
    x_s = x_sample.rearrange("b t d -> (b t) d")
    x_tiles = [x_p[j * P:(j + 1) * P] for j in range(NTILE - 1)] + [x_s]
    y_s = y_sample.rearrange("b t d -> (b t) d")
    y_tiles = [y_prompt[0][j * P:(j + 1) * P] for j in range(NTILE - 1)] + [y_s]
    win_v = w_in[0].rearrange("(k p) n -> p k n", p=P)
    wout_v = w_out[0].rearrange("(k p) n -> p k n", p=P)
    wup_v = w_up[0].rearrange("(k p) n -> p k n", p=P)
    wbp_v = w_branch_pool[0].rearrange("(k p) n -> p k n", p=P)
    wba_v = w_branch_attn[0].rearrange("(v c d) n -> v d c n", v=2, c=NQ)
    wdn_v = w_down[0].rearrange("(i k p) n -> p i k n", p=P, k=2)
    gates_dram = nc.dram_tensor("gates_scratch", [16, P, TP], F32).ap()

    with ExitStack() as ctx:
        free_at = [(nc.sbuf_base + 63) // 64 * 64]
        top = nc.sbuf_usable_end

        def region(nbytes):
            start = free_at[0]
            free_at[0] += (nbytes + 31) // 32 * 32
            assert free_at[0] <= top, (free_at[0], top)
            return start

        class Place:

            def __init__(self, start, size):
                self.at, self.end = start, start + size

            def __call__(self, name, shape, dt=F32):
                n = 4
                for d in shape[1:]:
                    n *= d
                t = nc.alloc_sbuf_tensor_at(name, [P] + shape[1:], dt, offset=self.at)
                self.at += (n + 31) // 32 * 32
                assert self.at <= self.end, (name, self.at - self.end)
                return t

        ROW = TP * 4
        REG_H = region(16 * ROW)
        REG_M = region(16 * ROW)
        REG_UP = region(16384)
        REG_RAW = region(8192)
        REG_DN = region(24576)
        REG_MISC = region(22400)

        at = Place(REG_UP, 16384)
        up_hi = at("up_hi", [P, 2, KD, P], F32R)
        up_lo = at("up_lo", [P, 2, KD, P], F32R)
        raw = Place(REG_RAW, 8192)("raw", [P, 2, KD, P])
        at = Place(REG_DN, 24576)
        dn_hi = at("dn_hi", [P, 2, D], F32R)
        dn_lo = at("dn_lo", [P, 2, D], F32R)
        raw_dn = at("raw_dn", [P, 2, D])

        at = Place(REG_MISC, 22400)
        ident = at("ident", [P, P])
        ones = at("ones", [P, P])
        mask = at("mask", [P, 2 * WIN])
        mask_first = at("mask_first", [P, 2 * WIN])
        smask = at("smask", [P, SKEYS])
        cols = at("cols", [P, 4 * 2 * NFF + KD + NG])
        cw = cols[:, 0:8 * NFF].rearrange("p (a c) -> p a c", a=4)
        gffn = cols[:, 8 * NFF:8 * NFF + KD]
        pscale = cols[:, 8 * NFF + KD:8 * NFF + KD + NG]
        cstate = at("cstate", [P, 2 * NFF, DEC_B * CSTATE])
        rcount = at("rcount", [P, 16])
        sink_b = at("sink_b", [P, 8])
        sink_s = at("sink_s", [P, 2])
        sink_t = at("sink_t", [P, 2])
        ssq = at("ssq", [P, NTILE])
        root = at("root", [P, NTILE])
        rstd = at("rstd", [P, NTILE])
        smx = at("smx", [P, 4])
        snegm = at("snegm", [P, 4])
        ssum = at("ssum", [P, 4])
        sesink = at("sesink", [P, 4])
        sden = at("sden", [P, 4])
        srec = at("srec", [P, 4])
        wgrp = at("wgrp", [P, NG, P])
        vnew_at = at.at
        vnew = at("vnew", [P, DEC_B, P])
        qblk_at = at.at
        qblk = at("qblk", [P, NQ, WIN])
        upack = at("upack", [P, NG, NSAMP])
        qpack = at("qpack", [P, DEC_B, NQ, DEC_T])
        tpack = at("tpack", [P, 2, CSTATE + 2 * DEC_B])
        x4_at = at.at

        tmp = Place(vnew_at, 6144)
        rms_row = tmp("rms_row", [P, TP])
        ssq2 = tmp("ssq2", [P, 2, NTILE])

        tmp = Place(qblk_at, 2048)
        rep8 = tmp("rep8", [P, 16, 8])
        rep4 = tmp("rep4", [P, 4, 4, 8])
        mask8 = tmp("mask8", [P, SKEYS])
        tmp = Place(x4_at, 4608)
        sprob = tmp("sprob", [P, 2, SKEYS])
        sprob_c = tmp("sprob_c", [P, 2, P])
        sprob_n = tmp("sprob_n", [P, 2, P])
        xcol1 = Place(x4_at, 4608)("xcol1", [P, NTILE, P])
        diag = Place(x4_at, 4608)("diag", [P, NTILE, P])
        conv_val = Place(x4_at, 4608)("conv_val", [P, EXT])

        at = Place(REG_H, 16 * ROW)
        h_hi = at("h_hi", [P, KD, TP], F32R)
        h_lo = at("h_lo", [P, KD, TP], F32R)
        at = Place(REG_H, 16 * ROW)
        ao_hi = at("ao_hi", [P, KD, TP], F32R)
        ao_lo = at("ao_lo", [P, KD, TP], F32R)
        at = Place(REG_H, 16 * ROW)
        y = at("y", [P, KD, TP])
        act_at = at.at
        act_hi = at("act_hi", [P, 2, TP], F32R)
        act_lo = at("act_lo", [P, 2, TP], F32R)
        ext_gate = at("ext_gate", [P, EXT])
        ext_val = at("ext_val", [P, EXT])
        conv_gate = at("conv_gate", [P, EXT])
        tail_rows = at("tail_rows", [P, 2, 2, P])
        at = Place(act_at, 4 * ROW)
        xsq = at("xsq", [P, 4, TP])
        xT, sq, sqsum = xsq[:, 0:2], xsq[:, 2], xsq[:, 3]

        at = Place(REG_M, 16 * ROW)
        xtok = at("xtok", [P, NTILE, D])
        at = Place(REG_M, 16 * ROW)
        uext = at("uext", [P, NG, UEXT])
        qT = at("qT", [P, NQ, TP])
        kT = at("kT", [P, WIN + TP])
        vT_at = at.at
        vT = at("vT", [P, TP])
        gmix_b = Place(vT_at, ROW)("gmix_b", [P, D])
        vtok_at = at.at
        vtok = at("vtok", [P, 1 + NBLK, P])
        cst = Place(vtok_at, 4608)("cst", [P, 6, P])
        kcT_at = at.at
        kcT = at("kcT", [P, DEC_B, WIN])
        sq_junk = Place(kcT_at, 4096)("sq_junk", [P, D])
        vc = at("vc", [P, DEC_B, P])
        prob_at = at.at
        prob = at("prob", [P, NQ, 2 * WIN])
        probT_at = at.at
        probT = at("probT", [P, 2, NQ * P])
        kblk = at("kblk", [P, 2 * WIN])
        vblk_at = at.at
        vblk = at("vblk", [P, 2, P])
        pst = Place(prob_at, 4096)("pst", [P, POOL_W])
        tmp = Place(prob_at, 4096)
        uout_p = tmp("uout_p", [P, POOL_W])
        uout_s = tmp("uout_s", [P, POOL_W])
        ktok = Place(probT_at, 4096)("ktok", [P, DEC_B, P])
        at = Place(REG_M, 16 * ROW)
        mx_hi = at("mx_hi", [P, KD, TP], F32R)
        mx_lo = at("mx_lo", [P, KD, TP], F32R)
        at = Place(REG_M, 16 * ROW)
        h2_hi = at("h2_hi", [P, KD, TP], F32R)
        h2_lo = at("h2_lo", [P, KD, TP], F32R)
        at = Place(REG_M, 16 * ROW)
        ytok = at("ytok", [P, NTILE, D])
        gfin_b = at("gfin_b", [P, D])
        ysq_junk = at("ysq_junk", [P, D // 2])

        convst = Place(REG_DN, 24576)("convst", [P, 2 * D_FF])
        at = Place(REG_DN, 24576)
        sum_a = at("sum_a", [P, UEXT])
        sum_b = at("sum_b", [P, UEXT])
        dT = at("dT", [P, TP])
        tmp = Place(REG_DN, 4892)
        kout_p = tmp("kout_p", [P, P])
        kout_s = tmp("kout_s", [P, P])
        gate_st = at("gate_st", [P, 2, TP])
        at = Place(REG_DN, 24576)
        gates = at("gates", [P, 2, 2, TP])
        xcol0 = at("xcol0", [P, NTILE, P])
        xcol = [xcol0, xcol1]

        PS = ctx.enter_context(nc.psum_tensor("PS", [P, 8, 512], F32))
        acc = [PS[:, 3 * s:3 * s + 3, 0:NP] for s in range(2)]
        aux = PS[:, 6:8, :].rearrange("p b n -> p (b n)")

        def sem(name):
            return ctx.enter_context(nc.semaphore(name))

        x_in = [sem(f"x_in{j}") for j in range(NTILE)]
        gmix_in, const_in, convst_in = sem("gmix_in"), sem("const_in"), sem("convst_in")
        raw_in = [sem("raw_in0"), sem("raw_in1")]
        dn_in = sem("dn_in")
        wgrp_in = sem("wgrp_in")
        u_out, kv_out = sem("u_out"), sem("kv_out")
        dram_copy = sem("dram_copy")
        gate_out = [sem("gate_out0"), sem("gate_out1")]
        gate_in = [sem("gate_in0"), sem("gate_in1")]
        xcol_in = [sem("xcol_in0"), sem("xcol_in1")]
        tail_out = sem("tail_out")
        sums_full, sums_added = sem("sums_full"), sem("sums_added")
        seg_scaled, seg_prod, seg_hi, seg_lo = sem("seg_scaled"), sem("seg_prod"), sem("seg_hi"), sem("seg_lo")
        ysq_done, yms_done, yroot_done = sem("ysq_done"), sem("yms_done"), sem("yroot_done")
        gfin_in = sem("gfin_in")
        y_out = sem("y_out")
        xt_full, acc_full, aux_full, mx_read = sem("xt_full"), sem("acc_full"), sem("aux_full"), sem("mx_read")
        h_read = sem("h_read")
        x_sq, x_root, x_hi = sem("x_sq"), sem("x_root"), sem("x_hi")
        w_hi, dn_hi_done = sem("w_hi"), sem("dn_hi_done")
        proj_done, exp_done, sexp_done = sem("proj_done"), sem("exp_done"), sem("sexp_done")
        ao_hi_done, mix_hi_done = sem("ao_hi_done"), sem("mix_hi_done")
        sq_done, root2, h2_hi_done = sem("sq_done"), sem("root2"), sem("h2_hi_done")
        states_in, tails_taken = sem("states_in"), sem("tails_taken")
        silu_done, act_hi_done = sem("silu_done"), sem("act_hi_done")
        x_ms, x_scaled, x_lo = sem("x_ms"), sem("x_scaled"), sem("x_lo")
        w_lo, dn_lo_done = sem("w_lo"), sem("dn_lo_done")
        d_done, smax_done, prob_done, ssmax_done, sprob_done = (sem("d_done"), sem("smax_done"), sem("prob_done"),
                                                                sem("ssmax_done"), sem("sprob_done"))
        acc_free = sem("acc_free")
        aux_free = sem("aux_free")
        ao_lo_done, mix_sum, mix_lo_done = sem("ao_lo_done"), sem("mix_sum"), sem("mix_lo_done")
        diag_done, h2_lo_done, up_scaled = sem("diag_done"), sem("h2_lo_done"), sem("up_scaled")
        conv_done, prod_done, act_lo_done = sem("conv_done"), sem("prod_done"), sem("act_lo_done")
        y_scaled = sem("y_scaled")
        dve_step = sem("dve_step")
        pool_step, const_done, uzero_done = sem("pool_step"), sem("const_done"), sem("uzero_done")
        qk_staged, v_staged, sq_added, pads_done = (sem("qk_staged"), sem("v_staged"), sem("sq_added"),
                                                               sem("pads_done"))
        u_packed = sem("u_packed")

        block = ctx.enter_context(nc.Block())

        def samples(t, first, width):
            skip = width - DEC_T
            return t[:, first:first + DEC_B * width].rearrange("p (b w) -> p b w", b=DEC_B)[:, :, skip:width]

        def hinted_loop(engine, times):
            return nc.Fori(0, times, engines=bass.OrderedEngineSet([engine]), hint_back_edge=True)

        def split_source(c):
            return raw[:, c % 2], up_hi[:, c % 2], up_lo[:, c % 2]

        @block.sync
        def _(sp):
            def load_chunk(c, half, views, wait=True):
                if wait:
                    sp.wait_ge(w_lo, c - 1)
                for n, (dst, src) in enumerate(views):
                    last = n == len(views) - 1
                    sp.dma_start(dst, src).then_inc(raw_in[half], 48 - 16 * n if last else 16)

            def in_views(c):
                r = raw[:, c % 2]
                if N_U <= c < N_U + N_Q:
                    base = POOL_W + (c - N_U) * HD
                    return [(r[:, :, v * HD:(v + 1) * HD], win_v[:, :, base + v * NQ * HD:base + v * NQ * HD + HD])
                            for v in range(2)]
                col = c * P if c < N_U else 2 * POOL_W + (P if c == CHUNK_V else 0)
                return [(r, win_v[:, :, col:col + P])]

            def gate_views(cg, half):
                col = cg * P + (2 * POOL_W + 2 * P)
                return [(raw[:, half], win_v[:, :, bass.ds(col, P)])]

            def branch_views(m, half):
                r = raw[:, half]
                c = bass.ds(m * P, P)
                return [(r[:, 0:4], wbp_v[:, :, c])] + [(r[v * HD:(v + 1) * HD, 4:8], wba_v[v][:, :, c]) for v in range(2)]

            def out_views(m, half):
                return [(raw[:, half], wout_v[:, :, bass.ds(m * P, P)])]

            def up_views(j, val):
                return [(raw[:, val], wup_v[:, :, bass.ds(j * P + val * D_FF, P)])]

            def load_x(j):
                sp.dma_start(xtok[0:TILE_ROWS[j], j, :], x_tiles[j]).then_inc(x_in[j], 16)

            load_x(0)
            sp.dma_start(gmix_b[:, :], g_mix.partition_broadcast(P).rearrange("p a d -> p (a d)")).then_inc(gmix_in, 16)
            load_x(1)
            load_x(2)
            load_chunk(0, 0, in_views(0), wait=False)
            for j in range(3, NTILE):
                load_x(j)
            load_chunk(1, 1, in_views(1), wait=False)
            cwv = conv_w[0].rearrange("a (c p) -> c a p", p=P)
            sp.dma_start(cst[0:2 * NFF, 0:3, :], cwv).then_inc(const_in, 16)
            sp.dma_start(cst[0:2 * NFF, 3, :], conv_b[0].rearrange("(c p) -> c p", p=P)).then_inc(const_in, 16)
            sp.dma_start(cst[0:KD, 4, :], g_ffn[0].rearrange("(c p) -> c p", p=P)).then_inc(const_in, 16)
            sp.dma_start(cst[0:NG, 5, :], pool_scale[0].rearrange("(c p) -> c p", p=P)).then_inc(const_in, 16)
            sp.dma_start(sink_b[:, :], sinks.partition_broadcast(P).rearrange("p a d -> p (a d)")).then_inc(const_in, 16)
            with nc.allow_non_contiguous_dma(reason="eight sink logits"):
                sp.dma_start(sink_t[0:NQ, :], sinks[0].rearrange("(v c) -> c v", v=2)).then_inc(const_in, 16)
            sp.dma_start(convst[0:16, :], state_conv[0].rearrange("b r c -> (b r) c")).then_inc(convst_in, 16)
            sp.dma_start(pst[0:DEC_B * PSTATE, :], state_pool[0].rearrange("b r c -> (b r) c")).then_inc(const_in, 16)
            sp.dma_start(ktok[:, :, :], cache_k[0].rearrange("b t v d -> t b (v d)")).then_inc(const_in, 16)
            sp.dma_start(vc[:, :, :], cache_v[0].rearrange("b t v d -> t b (v d)")).then_inc(const_in, 16)
            sp.dma_start(wgrp[:, :, :], w_pool_grp[0].rearrange("g c d -> c g d")).then_inc(wgrp_in, 16)
            sp.dma_start(pool_sample[0][:, 0:PSTATE - DEC_T], state_pool[0][:, DEC_T:PSTATE]).then_inc(dram_copy, 16)
            sp.dma_start(k_sample[0][:, 0:WIN - DEC_T], cache_k[0][:, DEC_T:WIN]).then_inc(dram_copy, 16)
            sp.dma_start(v_sample[0][:, 0:WIN - DEC_T], cache_v[0][:, DEC_T:WIN]).then_inc(dram_copy, 16)

            for c in range(2, CHUNK_GATE):
                load_chunk(c, c % 2, in_views(c))
            for cg in range(4):
                if cg == 0:
                    sp.wait_ge(aux_free, AUX_U + 1)
                    sp.dma_start(pool_prompt[0, 0], uout_p[0:PSTATE, :]).then_inc(u_out, 16)
                    for b in range(DEC_B):
                        sp.dma_start(pool_sample[0][b, PSTATE - DEC_T:PSTATE],
                                     uout_s[b * DEC_T:(b + 1) * DEC_T, :]).then_inc(u_out, 16)
                if cg == 2:
                    sp.wait_ge(aux_free, AUX_K + 1)
                    sp.dma_start(k_prompt[0, 0].rearrange("t v d -> t (v d)"), kout_p[:, :]).then_inc(kv_out, 16)
                    for b in range(DEC_B):
                        sp.dma_start(k_sample[0][b, WIN - DEC_T:WIN].rearrange("t v d -> t (v d)"),
                                     kout_s[b * DEC_T:(b + 1) * DEC_T, :]).then_inc(kv_out, 16)
                load_chunk(CHUNK_GATE + cg, cg % 2, gate_views(cg, cg % 2))
            sp.wait_ge(aux_free, AUX_VNEW + 1)
            sp.dma_start(v_prompt[0, 0].rearrange("t v d -> t (v d)"), vtok[:, NBLK, :]).then_inc(kv_out, 16)
            sp.dma_start(v_sample[0][:, WIN - DEC_T:WIN].rearrange("b t v d -> t b (v d)"),
                         vnew[0:DEC_T, :, :]).then_inc(kv_out, 16)

            def store_gate(cg, half):
                sp.wait_ge(proj_done, cg + (FILL_GATE + 1))
                sp.dma_start(gates_dram[cg], gate_st[:, half, :]).then_inc(gate_out[half], 16)

            with sp.Fori(0, 6) as n:
                for half in range(2):
                    store_gate(n * 2 + half, half)
                    load_chunk(n * 2 + (CHUNK_GATE + 4 + half), half, gate_views(n * 2 + (4 + half), half))
            def load_gates(m, half):
                sp.dma_start(gates[:, half, 0, :], gates_dram[m]).then_inc(gate_in[half], 16)
                sp.dma_start(gates[:, half, 1, :], gates_dram[m + KD]).then_inc(gate_in[half], 16)

            for cg in range(12, 16):
                store_gate(cg, cg % 2)
                load_chunk(CHUNK_BRANCH + cg - 12, cg % 2, branch_views(cg - 12, cg % 2))
                if cg == 14:
                    sp.wait_ge(gate_out[0], 16 * 5)
                    sp.wait_ge(kv_out, 16 * 11)
                    load_gates(0, 0)

            sp.wait_ge(gate_out[0], 16 * 8)
            sp.wait_ge(gate_out[1], 16 * 8)
            load_gates(1, 1)

            def load_xcol(m, half):
                c = bass.ds(m * P, P)
                sp.dma_start(xcol[half][:, 0:NTILE - 1, :], x_p.rearrange("(j p) d -> p j d", p=P)[:, :, c])\
                    .then_inc(xcol_in[half], 16)
                sp.dma_start(xcol[half][0:NSAMP, NTILE - 1, :], x_s[:, c]).then_inc(xcol_in[half], 16)

            load_xcol(0, 0)
            load_xcol(1, 1)
            for m in range(KD):
                if m < KD - 2:
                    sp.wait_ge(mix_lo_done, m + 1)
                    load_gates(m + 2, m % 2)
                c = CHUNK_BRANCH + m + 4
                if m < 4:
                    load_chunk(c, c % 2, branch_views(m + 4, m % 2))
                else:
                    load_chunk(c, c % 2, out_views(m - 4, m % 2))
            for m in range(KD):
                if m < KD - 2:
                    sp.wait_ge(aux_full, AUX_X + 2 * m + 2)
                    load_xcol(m + 2, m % 2)
                c = CHUNK_OUT + m + 4
                if m < 4:
                    load_chunk(c, c % 2, out_views(m + 4, m % 2))
                else:
                    load_chunk(c, c % 2, up_views((m - 4) // 2, m % 2))

            def load_down(i):
                sp.dma_start(raw_dn[:, :, :], wdn_v[:, i]).then_inc(dn_in, 16)

            sp.wait_ge(mix_lo_done, KD)
            sp.wait_ge(aux_full, AUX_X + 2 * KD)
            load_down(0)

            def store_tails(i):
                sp.wait_ge(aux_free, i * 4 + (AUX_TAIL + 4))
                for v in range(2):
                    c = bass.ds(i * (2 * P) + v * D_FF, 2 * P)
                    sp.dma_start(conv_prompt[0, 0][:, c], tail_rows[0:CSTATE, v, :, :].rearrange("r e p -> r (e p)"))\
                        .then_inc(tail_out, 16)
                    sp.dma_start(conv_sample[0].rearrange("b r c -> (b r) c")[:, c],
                                 tail_rows[CSTATE:CSTATE + 16, v, :, :].rearrange("r e p -> r (e p)")).then_inc(tail_out, 16)

            with sp.Fori(0, NFF // 2 - 1) as i:
                for e in range(2):
                    for val in range(2):
                        load_chunk(i * 4 + (CHUNK_UP + 4 + 2 * e + val), val, up_views(i * 2 + (2 + e), val))
                sp.wait_ge(dn_lo_done, i + 1)
                load_down(i + 1)
                store_tails(i)
            sp.wait_ge(acc_full, FILL_FFN + 12 * (NFF // 2 - 1) + 4)
            sp.dma_start(gfin_b[:, :], g_final.partition_broadcast(P)).then_inc(gfin_in, 16)
            store_tails(NFF // 2 - 1)
            for j in range(NTILE):
                sp.wait_ge(y_scaled, j + 1)
                sp.dma_start(y_tiles[j], ytok[0:TILE_ROWS[j], j, :]).then_inc(y_out, 16)
            sp.wait_ge(dram_copy, 16 * 3)
            sp.wait_ge(u_out, 16 * 9)
            sp.wait_ge(kv_out, 16 * 11)
            sp.wait_ge(tail_out, 16 * 4 * (NFF // 2))
            sp.wait_ge(y_out, 16 * NTILE)

        @block.tensor
        def _(pe):
            def gemm(s, c, first_k, ks, rhs_hi, rhs_lo, hooks=None, ready=None, read=None, cuts=THIRDS):
                _, w_h, w_l = split_source(c)
                for n, k in enumerate(ks):
                    if ready:
                        ready(k)
                    for q, (w, x) in enumerate(((w_h, rhs_hi), (w_h, rhs_lo), (w_l, rhs_hi))):
                        if hooks and 3 * n + q in hooks:
                            hooks[3 * n + q]()
                        for piece, (first, width) in enumerate(cuts):
                            ins = pe.matmul(PS[:, 3 * s + piece, 0:width], w[:, first_k + n, :],
                                            x[:, k, first:first + width],
                                            start=(n == 0 and q == 0), stop=(n == len(ks) - 1 and q == 2))
                    if read and n < len(ks) - 1:
                        ins.then_inc(read, 1)
                ins.then_inc(acc_full, 1)

            def aux_round(rnd, emit):
                pe.wait_ge(aux_free, rnd)
                emit().then_inc(aux_full, 1)

            def first_fill(piece, hooks={}):
                for k in range(KD):
                    if 3 * k in hooks:
                        hooks[3 * k]()
                    for q, (w, x) in enumerate(((up_hi, h_hi), (up_hi, h_lo), (up_lo, h_hi))):
                        ins = pe.matmul(acc[0][:, piece, :], w[:, 0, k, :], x[:, k, piece * NP:(piece + 1) * NP],
                                        start=(k == 0 and q == 0), stop=(k == KD - 1 and q == 2))
                return ins

            pe.wait_ge(const_done, 1)
            for j in range(NTILE):
                rows = TILE_ROWS[j]
                pe.wait_ge(x_scaled, j + 1)
                if j >= 3:
                    pe.wait_ge(x_lo, j - 2)
                for k in range(KD):
                    b = X_BANK + 2 * (j % 3) + k // 4
                    ins = pe.transpose(PS[:, b, (k % 4) * P:(k % 4) * P + rows], xtok[0:rows, j, k * P:(k + 1) * P],
                                       ident[0:rows, 0:rows])
                ins.then_inc(xt_full, 1)
                if j == 7:
                    pe.wait_ge(w_lo, 1)
                    pe.wait_ge(x_lo, 3)
                    first_fill(0)
                if j == 8:
                    pe.wait_ge(x_lo, 6)
                    first_fill(1)

            def turn_consts():
                pe.wait_ge(const_in, 16 * 9)
                nch = 2 * NFF
                for a in range(4):
                    pe.transpose(aux[:, a * nch:(a + 1) * nch], cst[0:nch, a, :], ident[0:nch, 0:nch])
                pe.transpose(aux[:, 4 * nch:4 * nch + KD], cst[0:KD, 4, :], ident[0:KD, 0:KD])
                pe.transpose(aux[:, 4 * nch + KD:4 * nch + KD + NG], cst[0:NG, 5, :], ident[0:NG, 0:NG])
                pe.matmul(aux[:, 512:512 + SKEYS], rep8[0:8].rearrange("p a b -> p (a b)"), mask8[0:8, :],
                          start=True, stop=True)
                return pe.matmul(aux[:, 768:770], rep4[0:4].rearrange("p a b c -> p (a b c)"), sink_t[0:4, :],
                                 start=True, stop=True)

            def turn_conv_states():
                pe.wait_ge(convst_in, 16)
                for c in range(2 * NFF):
                    ins = pe.transpose(aux[:, c * 16:(c + 1) * 16], convst[0:16, c * P:(c + 1) * P], ident[0:16, 0:16])
                return ins

            def turn_pool_states():
                n = DEC_B * PSTATE
                for g in range(NG):
                    ins = pe.transpose(aux[:, g * P:g * P + n], pst[0:n, g * P:(g + 1) * P], ident[0:n, 0:n])
                return ins

            def turn_cached_k():
                for b in range(DEC_B):
                    ins = pe.transpose(aux[:, b * P:(b + 1) * P], ktok[:, b, :], ident[:, :])
                return ins

            def turn_u():
                pe.wait_ge(proj_done, 4)
                pe.wait_ge(u_packed, 1)
                for g in range(NG):
                    pe.transpose(aux[0:PSTATE, g * P:(g + 1) * P], uext[:, g, SEQ:SEQ + PSTATE], ident[:, :])
                for g in range(NG):
                    ins = pe.transpose(aux[0:NSAMP, 512 + g * P:512 + (g + 1) * P], upack[:, g, :], ident[:, :])
                return ins

            def turn_k():
                pe.wait_ge(proj_done, 13)
                pe.transpose(aux[:, 0:P], kT[:, SEQ:SEQ + WIN], ident[:, :])
                return pe.transpose(aux[0:NSAMP, 512:512 + P], kT[:, WIN + SEQ:WIN + T], ident[:, :])

            def turn_v():
                pe.wait_ge(proj_done, 11)
                for n in range(NBLK):
                    ins = pe.transpose(aux[:, n * P:(n + 1) * P], vT[:, n * P:(n + 1) * P], ident[:, :])
                return ins

            def turn_new_v():
                for b in range(DEC_B):
                    ins = pe.transpose(aux[0:DEC_T, b * P:(b + 1) * P],
                                       vT[:, SEQ + b * DEC_T:SEQ + (b + 1) * DEC_T], ident[:, :])
                return ins

            early = {0: {12: (AUX_CONST, turn_consts)}, 1: {12: (AUX_CONV, turn_conv_states)},
                     2: {12: (AUX_POOL, turn_pool_states)}, 3: {12: (AUX_KC, turn_cached_k)},
                     5: {12: (AUX_U, turn_u)}, 12: {15: (AUX_V, turn_v), 23: (AUX_VNEW, turn_new_v)}}
            for f, (kind, n) in enumerate(ENTRIES):
                if f >= 2:
                    pe.wait_ge(proj_done, f - 1)
                if kind == "pool":
                    pe.wait_ge(d_done, n + 1)
                    if n == 0:
                        pe.wait_ge(wgrp_in, 16)
                    for piece in range(3):
                        ins = pe.matmul(acc[f % 2][:, piece, :], wgrp[:, n, :], dT[:, piece * NP:(piece + 1) * NP],
                                        start=True, stop=True)
                    ins.then_inc(acc_full, 1)
                    continue
                c = FIRST_CHUNK[kind] + n
                if c == 0:
                    pe.wait_ge(x_lo, NTILE)
                    pe.wait_ge(const_done, 2)
                hooks = {k: (lambda r=r, e=e: aux_round(r, e)) for k, (r, e) in early.get(f, {}).items()}
                if c == 0:
                    first_fill(2, hooks).then_inc(acc_full, 1)
                    continue
                pe.wait_ge(w_lo, c + 1)
                gemm(f % 2, c, 0, range(KD), h_hi, h_lo, hooks)
            aux_round(AUX_K, turn_k)

            def scores(n, kv):
                v = slice(kv * HD, (kv + 1) * HD)

                def emit():
                    pe.wait_ge(qk_staged, n + 1)
                    for c in range(NQ):
                        ins = pe.matmul(aux[:, c * 2 * WIN:(c + 1) * 2 * WIN], qblk[v, c, :], kblk[v, :],
                                        start=True, stop=True)
                    return ins
                return emit

            def turn_probs(s):
                def emit():
                    pe.wait_ge(prob_done, s + 1)
                    for b in range(2):
                        for c in range(NQ):
                            ins = pe.transpose(aux[:, (b * NQ + c) * P:(b * NQ + c + 1) * P],
                                               prob[:, c, b * WIN:(b + 1) * WIN], ident[:, :])
                    return ins
                return emit

            def values(n, kv):
                v = slice(kv * HD, (kv + 1) * HD)

                def emit():
                    pe.wait_ge(v_staged, n + 1)
                    for b in range(2):
                        ins = pe.matmul(aux[v, 0:NQ * P], vblk[:, b, v], probT[:, b, :], start=(b == 0), stop=(b == 1))
                    return ins
                return emit

            def sample_scores(h):
                def emit():
                    for kv in range(2):
                        v = slice(kv * HD, (kv + 1) * HD)
                        for i in range(4):
                            b = 4 * h + i
                            q = qpack[v, b].rearrange("p c t -> p (c t)")
                            rows = slice(32 * i, 32 * i + 32)
                            pe.matmul(aux[rows, kv * 512:kv * 512 + WIN], q, kcT[v, b, :], start=True, stop=True)
                            ins = pe.matmul(aux[rows, kv * 512 + WIN:kv * 512 + SKEYS], q,
                                            kT[v, WIN + SEQ + b * DEC_T:WIN + SEQ + (b + 1) * DEC_T],
                                            start=True, stop=True)
                    return ins
                return emit

            def sample_turn(h):
                def emit():
                    pe.wait_ge(sprob_done, h + 1)
                    for kv in range(2):
                        pe.transpose(aux[:, kv * 512:kv * 512 + P], sprob[:, kv, 0:WIN], ident[:, :])
                        ins = pe.transpose(aux[0:DEC_T, kv * 512 + P:kv * 512 + 2 * P], sprob[:, kv, WIN:SKEYS],
                                           ident[:, :])
                    return ins
                return emit

            def sample_values(h):
                def emit():
                    for kv in range(2):
                        v = slice(kv * HD, (kv + 1) * HD)
                        for i in range(4):
                            b = 4 * h + i
                            col = slice(32 * i, 32 * i + 32)
                            out = aux[v, kv * 512 + 32 * i:kv * 512 + 32 * i + 32]
                            pe.matmul(out, vc[:, b, v], sprob_c[:, kv, col], start=True, stop=False)
                            ins = pe.matmul(out, vnew[0:DEC_T, b, v], sprob_n[0:DEC_T, kv, col], start=False, stop=True)
                    return ins
                return emit

            def gate_block(n, first, last):
                for kv in range(2):
                    s = n * 2 + kv
                    c = CHUNK_GATE + kv
                    pe.wait_ge(w_lo, n * 2 + (c + 1))
                    pe.wait_ge(proj_done, n * 2 + (FILL_GATE + kv - 1))
                    hooks = {}

                    def at_k(k, rnd, emit):
                        before = hooks.get(k)

                        def run():
                            if before:
                                before()
                            aux_round(rnd, emit)
                        hooks[k] = run
                    if first:
                        r_s, r_t, r_v = AUX_SAMPLE[kv]
                        at_k(6, r_s, sample_scores(kv))
                        at_k(14, aux_turn(s), turn_probs(s))
                        at_k(17, aux_values(s), values(n, kv))
                        at_k(19, r_t, sample_turn(kv))
                        at_k(21, r_v, sample_values(kv))
                    else:
                        at_k(15, aux_turn(s), turn_probs(s))
                        at_k(18, aux_values(s), values(n, kv))
                    next_scores = 23 if first else 21
                    if kv == 0:
                        at_k(next_scores, aux_scores(s + 1), scores(n, 1))
                    elif not last:
                        at_k(next_scores, aux_scores(s + 1), scores(n + 1, 0))
                    gemm(kv, c, 0, range(KD), h_hi, h_lo, hooks, read=h_read if last and kv else None)

            aux_round(aux_scores(0), scores(0, 0))
            gate_block(0, True, False)
            with pe.Fori(0, 6) as i:
                gate_block(i + 1, False, False)
            gate_block(7, False, True)

            def branch(m, half, ready=None):
                c = CHUNK_BRANCH + half
                pe.wait_ge(w_lo, m + (CHUNK_BRANCH + 1))
                if not ready:
                    pe.wait_ge(acc_free, m * 2 - 1)
                gemm(0, c, 0, range(0, 4), ao_hi, ao_lo, ready=ready)
                if ready:
                    pe.wait_ge(proj_done, FILL_BRANCH)
                else:
                    pe.wait_ge(acc_free, m * 2)
                gemm(1, c, 4, range(4, 8), ao_hi, ao_lo, ready=ready)

            pe.wait_ge(proj_done, FILL_BRANCH - 1)
            branch(0, 0, ready=lambda k: pe.wait_ge(ao_lo_done, k + 1))
            branch(1, 1)
            with pe.Fori(0, 3) as i:
                branch(i * 2 + 2, 0)
                branch(i * 2 + 3, 1)

            def project(m, half, ready=None, read=None):
                pe.wait_ge(w_lo, m + (CHUNK_OUT + 1))
                pe.wait_ge(acc_free, m + (FILL_OUT - 1) - FILL_BRANCH)

                def turn_x():
                    pe.wait_ge(xcol_in[half], (m - half) * 16 + 32)
                    for j in range(NTILE - 2):
                        ins = pe.transpose(aux[:, j * P:(j + 1) * P], xcol[half][:, j, :], ident[:, :])
                    return ins

                def turn_x_last():
                    pe.transpose(aux[:, 0:P], xcol[half][:, NTILE - 2, :], ident[:, :])
                    return pe.transpose(aux[:, P:P + NSAMP], xcol[half][0:NSAMP, NTILE - 1, :], ident[0:NSAMP, 0:NSAMP])

                gemm(half, CHUNK_OUT + half, 0, range(KD), mx_hi, mx_lo,
                     {3: lambda: aux_round(m * 2 + AUX_X, turn_x), 15: lambda: aux_round(m * 2 + (AUX_X + 1), turn_x_last)},
                     ready, read)

            project(0, 0, ready=lambda k: pe.wait_ge(mix_lo_done, k + 1))
            project(1, 1)
            with pe.Fori(0, 2) as i:
                project(i * 2 + 2, 0)
                project(i * 2 + 3, 1)
            project(KD - 2, 0)
            project(KD - 1, 1, read=mx_read)

            def token_squares():
                def emit():
                    pe.wait_ge(sq_added, KD)
                    for j, rows in enumerate(TILE_ROWS):
                        ins = pe.matmul(aux[0:rows, j:j + 1], sqsum[:, j * P:j * P + rows], ones[:, 0:1],
                                        start=True, stop=True)
                    return ins
                aux_round(AUX_SSQ, emit)

            def spread_rms(part):
                def emit():
                    pe.wait_ge(diag_done, 1)
                    for j in range(NTILE - 1) if part == 0 else [NTILE - 1]:
                        ins = pe.matmul(aux[:, (j % 8) * P:(j % 8) * P + TILE_ROWS[j]], ones[:, :],
                                        diag[:, j, 0:TILE_ROWS[j]], start=True, stop=True)
                    return ins
                aux_round(AUX_RMS + part, emit)

            def turn_tails(i, e, val):
                def emit():
                    pe.wait_ge(tails_taken, i * 4 + (2 * e + val + 1))
                    return pe.transpose(aux[0:CSTATE + 16, 0:P], tpack[:, val, :], ident[:, :])
                return lambda: aux_round(i * 4 + (AUX_TAIL + 2 * e + val), emit)

            def up(c, s, i, add, hooks, ready=None, cuts=THIRDS):
                pe.wait_ge(w_lo, i * 4 + (CHUNK_UP + add + 1))
                gemm(s, c, 0, range(KD), h2_hi, h2_lo, hooks, ready, cuts=cuts)

            def down(i):
                pe.wait_ge(dn_lo_done, i + 1)
                pe.wait_ge(act_lo_done, i * 2 + 2)
                for m in range(KD):
                    if m < 2:
                        pe.wait_ge(up_scaled, i * 4 + (4 + m))
                    else:
                        pe.wait_ge(acc_free, i * 8 + (FILL_FFN - FILL_BRANCH + m - 1))
                    for e in range(2):
                        for q, (w, x) in enumerate(((dn_hi, act_hi), (dn_hi, act_lo), (dn_lo, act_hi))):
                            for piece, (first, width) in enumerate(THIRDS):
                                ins = pe.matmul(acc[1 - m % 2][:, piece, 0:width], w[:, e, m * P:(m + 1) * P],
                                                x[:, e, first:first + width],
                                                start=(e == 0 and q == 0), stop=(e == 1 and q == 2))
                    ins.then_inc(acc_full, 1)

            def last_down(i, hooks):
                def half(p, m, e):
                    first, width = SEGS[p]
                    for q, (w, x) in enumerate(((dn_hi, act_hi), (dn_hi, act_lo), (dn_lo, act_hi))):
                        ins = pe.matmul(PS[:, (p * KD + m) % 6, 0:width], w[:, e, m * P:(m + 1) * P],
                                        x[:, e, first:first + width], start=(e == 0 and q == 0),
                                        stop=(e == 1 and q == 2))
                    return ins

                pe.wait_ge(dn_lo_done, i + 1)
                pe.wait_ge(act_lo_done, i * 2 + 1)
                pe.wait_ge(up_scaled, i * 4 + 3)
                for m in range(6):
                    if m >= 3:
                        pe.wait_ge(seg_scaled, m - 2)
                    half(0, m, 0)
                for p in range(3):
                    pe.wait_ge(seg_lo, p + 1)
                    for m in range(KD):
                        f = p * KD + m
                        if f >= 6:
                            pe.wait_ge(sums_added, f - 5)
                            half(p, m, 0)
                        half(p, m, 1).then_inc(sums_full, 1)
                        if f in hooks:
                            hooks[f]()

            def ffn(i, last):
                base = FILL_FFN - FILL_BRANCH
                pe.wait_ge(acc_free, i * 8 + (base - 1))
                up(1, 1, i, 1, {9: turn_tails(i, 0, 0)})
                pe.wait_ge(acc_free, i * 8 + base)
                pe.wait_ge(up_scaled, i * 4 + 1)
                up(0, 0, i, 2, {9: turn_tails(i, 0, 1)})
                pe.wait_ge(up_scaled, i * 4 + 2)
                up(1, 1, i, 3, {9: turn_tails(i, 1, 0)}, cuts=SEGS if last else THIRDS)
                if not last:
                    pe.wait_ge(up_scaled, i * 4 + 3)
                    up(0, 0, i, 4, {9: turn_tails(i, 1, 1)})
                    down(i)

            pe.wait_ge(acc_free, FILL_FFN - FILL_BRANCH - 1)
            up(0, 0, 0, 0, {12: token_squares, 22: lambda: spread_rms(0)}, ready=lambda k: pe.wait_ge(h2_lo_done, k + 1))
            spread_rms(1)
            with hinted_loop(mybir.EngineType.PE, NFF // 2 - 1) as i:
                ffn(i, False)
            i = NFF // 2 - 1
            ffn(i, True)

            def turn_y(r):
                p, m = r // 4, r % 4 * 2

                def emit():
                    pe.wait_ge(sums_added, p * KD + m + 2)
                    for h in range(2):
                        for n, j in enumerate(range(3 * p, 3 * p + 3)):
                            rows = TILE_ROWS[j]
                            ins = pe.transpose(aux[0:rows, (4 * h + n) * P:(4 * h + n + 1) * P],
                                               y[:, m + h, j * P:j * P + rows], ident[:, :])
                    return ins
                return lambda: aux_round(AUX_Y + r, emit)

            hooks = {p * KD + 2 * q + 5: turn_y(4 * p + q) for p in range(3) for q in range(4)}
            hooks[3] = turn_tails(i, 1, 1)
            last_down(i, hooks)
            turn_y(10)()
            turn_y(11)()

        def x_banks(j, rows):
            b = X_BANK + 2 * (j % 3)
            return PS[:, b:b + 2, :].rearrange("p b (k t) -> p (b k) t", k=4)[:, :, 0:rows]

        def copy_pieces(copy, dst, first, samp, width, s):
            copy(dst[:, first:first + 2 * NP].rearrange("p (a n) -> p a n", a=2), acc[s][:, 0:2, :])
            copy(dst[:, first + 2 * NP:first + SEQ], acc[s][:, 2, 0:SEQ - 2 * NP])
            return copy(samples(dst, samp, width),
                        acc[s][:, 2, SEQ - 2 * NP:T - 2 * NP].rearrange("p (b t) -> p b t", b=DEC_B))

        def pieces(t):
            return t.rearrange("p (a n) -> p a n", a=3)

        def take_y(eng, copy, r):
            p, m = r // 4, r % 4 * 2
            full = 3 if p < 2 else 2
            turned = aux[:, :].rearrange("p (m j f) -> p j m f", m=2, j=4)
            cols_m = slice(m * P, (m + 2) * P)
            eng.wait_ge(aux_full, AUX_Y + r + 1)
            ins = copy(ytok[:, 3 * p:3 * p + full, cols_m].rearrange("p j (m f) -> p j m f", m=2), turned[:, 0:full])
            if full == 2:
                ins = copy(ytok[0:NSAMP, NTILE - 1, cols_m].rearrange("p (m f) -> p m f", m=2), turned[0:NSAMP, 2])
            ins.then_inc(aux_free, 1)

        @block.scalar
        def _(act):
            def copy(dst, src):
                return act.activation(dst, src, ACT.Copy)

            def split_hi(half, pair):
                act.wait_ge(raw_in[half], landed(pair))
                copy(up_hi[:, half], raw[:, half]).then_inc(w_hi, 1)

            def x_split(j):
                rows = TILE_ROWS[j]
                act.wait_ge(xt_full, j + 1)
                copy(h_hi[:, :, j * P:j * P + rows], x_banks(j, rows)).then_inc(x_hi, 1)

            act.wait_ge(const_done, 1)
            def x_squares(*tiles):
                for j in tiles:
                    rows = TILE_ROWS[j]
                    act.wait_ge(x_in[j], 16)
                    if j:
                        act.wait_ge(x_sq, j)
                    act.activation(sq_junk[0:rows, :], xtok[0:rows, j, :], ACT.Square, accum_out=ssq[0:rows, j:j + 1])\
                        .then_inc(x_sq, 1)

            def x_roots(g):
                tiles = slice(*X_GROUPS[g])
                act.wait_ge(x_ms, g + 1)
                act.activation(root[:, tiles], ssq[:, tiles], ACT.Sqrt).then_inc(x_root, 1)

            act.activation(smx[:, 0:1], ones[:, 0:1], ACT.Sqrt)
            x_squares(0)
            x_roots(0)
            x_squares(1, 2)
            x_roots(1)
            x_split(0)
            x_squares(3, 4, 5)
            x_roots(2)
            x_split(1)
            x_split(2)
            x_squares(6, 7, 8)
            x_roots(3)
            x_split(3)
            split_hi(0, 0)
            for j in range(4, NTILE):
                x_split(j)
            split_hi(1, 0)

            for f, (kind, n) in enumerate(ENTRIES):
                act.wait_ge(acc_full, f + 1)
                if kind == "u":
                    ins = copy_pieces(copy, uext[:, n, :], PSTATE, USAMP, PSTATE + DEC_T, f % 2)
                elif kind == "q":
                    ins = copy(pieces(qT[:, n, :]), acc[f % 2])
                elif kind == "k":
                    ins = copy(pieces(kT[:, WIN:WIN + TP]), acc[f % 2])
                elif kind == "v":
                    ins = copy(pieces(vT[:, :]), acc[f % 2])
                else:
                    ins = act.activation(pieces(uext[:, n, 0:TP]), acc[f % 2], ACT.Copy, scale=pscale[:, n:n + 1])
                ins.then_inc(proj_done, 1)
                if kind != "pool":
                    c = FIRST_CHUNK[kind] + n + 2
                    split_hi(c % 2, c - c % 2)

            def exps(s):
                act.wait_ge(smax_done, s + 1)
                for c in range(NQ):
                    act.activation(prob[:, c, :], prob[:, c, :], ACT.Exp, bias=snegm[:, c:c + 1],
                                   accum_out=ssum[:, c:c + 1])
                act.activation(sesink[:, :], sesink[:, :], ACT.Exp).then_inc(exp_done, 1)

            def sample_exps(h):
                act.wait_ge(ssmax_done, h + 1)
                for kv in range(2):
                    act.activation(sprob[:, kv, :], sprob[:, kv, :], ACT.Exp, bias=snegm[:, kv:kv + 1],
                                   accum_out=ssum[:, kv:kv + 1])
                act.activation(sesink[:, 0:2], sesink[:, 0:2], ACT.Exp).then_inc(sexp_done, 1)

            def gate_block(n, first, last):
                for kv in range(2):
                    if first:
                        sample_exps(kv)
                    if not (last and kv):
                        exps(n * 2 + (kv + 1))
                    else:
                        for k in range(4):
                            branch_input(k)
                    act.wait_ge(acc_full, n * 2 + (FILL_GATE + kv + 1))
                    if not first:
                        act.wait_ge(gate_out[kv], n * 16)
                    act.activation(pieces(gate_st[:, kv, :]), acc[kv], ACT.Sigmoid).then_inc(proj_done, 1)
                    split_hi(kv, n * 2 + (CHUNK_GATE + 2))

            def branch_input(k):
                if k < KD - 1:
                    act.wait_ge(h_read, k + 1)
                copy(ao_hi[:, k, :], uext[:, k, 0:TP] if k < 4 else qT[:, k - 4, :]).then_inc(ao_hi_done, 1)

            exps(0)
            gate_block(0, True, False)
            with act.Fori(0, 6) as i:
                gate_block(i + 1, False, False)
            gate_block(7, False, True)
            act.wait_ge(aux_free, AUX_X)
            for k in range(4, KD):
                branch_input(k)

            def mix(m, half):
                act.wait_ge(mix_sum, m + 1)
                copy(mx_hi[:, bass.ds(m, 1), :], gates[:, half, 0:1, :]).then_inc(mix_hi_done, 1)
                split_hi(half, (m - half) + (CHUNK_BRANCH + 2))

            with act.Fori(0, 4) as i:
                for half in range(2):
                    mix(i * 2 + half, half)

            act.wait_ge(pads_done, 1)

            def project(m, half, last=False, between={}):
                act.wait_ge(aux_full, m * 2 + (AUX_X + 1))
                act.wait_ge(acc_free, m + (FILL_OUT - FILL_BRANCH - 1))
                copy(xT[:, half, 0:SEQ - P], aux[:, 0:SEQ - P]).then_inc(aux_free, 1)
                if last:
                    between[1]()
                act.wait_ge(aux_full, m * 2 + (AUX_X + 2))
                copy(xT[:, half, SEQ - P:T], aux[:, 0:P + NSAMP]).then_inc(aux_free, 1)
                if last:
                    between[2]()
                act.wait_ge(acc_free, m + (FILL_OUT - FILL_BRANCH + 1))
                act.wait_ge(sq_added, m)
                act.activation(sq[:, :].unsqueeze(1), y[:, bass.ds(m, 1), :], ACT.Square).then_inc(sq_done, 1)
                if not last:
                    split_hi(half, (m - half) + (CHUNK_OUT + 2))

            with act.Fori(0, 3) as i:
                for half in range(2):
                    project(i * 2 + half, half)
            project(KD - 2, 0)

            def ffn_input(k):
                act.wait_ge(acc_free, FILL_OUT - FILL_BRANCH + k + 1)
                if k < KD - 1:
                    act.wait_ge(mx_read, k + 1)
                act.activation(h2_hi[:, k, :], y[:, k, :], ACT.Copy, scale=gffn[:, k:k + 1]).then_inc(h2_hi_done, 1)

            project(KD - 1, 1, True, {1: lambda: [ffn_input(k) for k in range(4)], 2: lambda: [ffn_input(4), ffn_input(5)]})
            ffn_input(6)
            ffn_input(7)
            split_hi(1, CHUNK_UP)
            act.wait_ge(aux_free, AUX_SSQ + 1)
            act.activation(root[:, :], ssq[:, :], ACT.Sqrt).then_inc(root2, 1)

            def up_edges(val, u, ch):
                act.wait_ge(conv_done, u)
                ext = ext_val if val else ext_gate
                seqs = ext[:, ESAMP:EXT].rearrange("p (b w) -> p b w", b=DEC_B)
                copy(seqs[:, :, 0:CSTATE], cstate[:, bass.ds(ch, 1), :].rearrange("p o (b w) -> p (o b) w", b=DEC_B))\
                    .then_inc(states_in, 1)
                act.wait_ge(up_scaled, u + 1)
                copy(tpack[:, val, 0:CSTATE], ext[:, SEQ:SEQ + CSTATE])
                copy(tpack[:, val, CSTATE:].rearrange("p (b w) -> p b w", b=DEC_B), seqs[:, :, DEC_T:DEC_T + CSTATE])\
                    .then_inc(tails_taken, 1)

            def silu(j, u1):
                act.wait_ge(conv_done, u1)
                act.activation(conv_gate[:, 0:NCONV], conv_gate[:, 0:NCONV], ACT.Silu).then_inc(silu_done, 1)

            def act_split(j, e):
                act.wait_ge(prod_done, j + 1)
                act.wait_ge(pads_done, 2)
                copy(act_hi[:, e, 0:SEQ], conv_val[:, 0:SEQ])
                copy(act_hi[:, e, SEQ:T].rearrange("p (b t) -> p b t", b=DEC_B),
                     samples(conv_val, ESAMP - CSTATE, CSTATE + DEC_T)).then_inc(act_hi_done, 1)

            def tails(i, e, val):
                act.wait_ge(aux_full, i * 4 + (AUX_TAIL + 2 * e + val + 1))
                copy(tail_rows[0:CSTATE + 16, val, e, :], aux[0:CSTATE + 16, 0:P]).then_inc(aux_free, 1)

            up_edges(0, 0, 0)
            split_hi(0, CHUNK_UP + 2)
            silu(0, 1)

            def ffn(i, last):
                act.wait_ge(tail_out, i * 64)
                tails(i, 0, 0)
                up_edges(1, i * 4 + 1, i * 2 + NFF)
                split_hi(1, i * 4 + (CHUNK_UP + 2))
                act.wait_ge(dn_in, i * 16 + 16)
                copy(dn_hi[:, :, :], raw_dn[:, :, :]).then_inc(dn_hi_done, 1)
                act_split(i * 2, 0)
                tails(i, 0, 1)
                up_edges(0, i * 4 + 2, i * 2 + 1)
                if not last:
                    split_hi(0, i * 4 + (CHUNK_UP + 4))
                silu(i * 2 + 1, i * 4 + 3)
                tails(i, 1, 0)
                if not last:
                    up_edges(1, i * 4 + 3, i * 2 + (NFF + 1))
                    split_hi(1, i * 4 + (CHUNK_UP + 4))
                    act_split(i * 2 + 1, 1)
                    tails(i, 1, 1)
                    up_edges(0, i * 4 + 4, i * 2 + 2)
                    split_hi(0, i * 4 + (CHUNK_UP + 6))
                    silu(i * 2 + 2, i * 4 + 5)

            with hinted_loop(mybir.EngineType.Activation, NFF // 2 - 1) as i:
                ffn(i, False)
            i = NFF // 2 - 1
            ffn(i, True)

            def seg_split(p):
                first, width = SEGS[p]
                act.wait_ge(seg_prod, p + 1)
                if p < 2:
                    copy(act_hi[:, 1, first:first + width], conv_val[:, first:first + width]).then_inc(seg_hi, 1)
                else:
                    copy(act_hi[:, 1, first:SEQ], conv_val[:, first:SEQ])
                    copy(act_hi[:, 1, SEQ:T].rearrange("p (b t) -> p b t", b=DEC_B),
                         samples(conv_val, ESAMP - CSTATE, CSTATE + DEC_T)).then_inc(seg_hi, 1)

            act.wait_ge(conv_done, i * 4 + 3)
            seqs = ext_val[:, ESAMP:EXT].rearrange("p (b w) -> p b w", b=DEC_B)
            copy(seqs[:, :, 0:CSTATE], cstate[:, 2 * NFF - 1, :].rearrange("p (b w) -> p b w", b=DEC_B))\
                .then_inc(states_in, 1)
            seg_split(0)
            act.wait_ge(seg_scaled, 3)
            copy(tpack[:, 1, 0:CSTATE], ext_val[:, SEQ:SEQ + CSTATE])
            copy(tpack[:, 1, CSTATE:].rearrange("p (b w) -> p b w", b=DEC_B), seqs[:, :, DEC_T:DEC_T + CSTATE])\
                .then_inc(tails_taken, 1)
            seg_split(1)
            tails(i, 1, 1)
            take_y(act, copy, 0)
            seg_split(2)

            def y_squares(p, part):
                feats = slice(part * D // 2, (part + 1) * D // 2)
                act.wait_ge(aux_free, AUX_Y + 4 * p + 2 * part + 2)
                for n, j in enumerate(range(3 * p, 3 * p + 3)):
                    rows = TILE_ROWS[j]
                    if 6 * p + 3 * part + n:
                        act.wait_ge(ysq_done, 6 * p + 3 * part + n)
                    act.activation(ysq_junk[0:rows, :], ytok[0:rows, j, feats], ACT.Square,
                                   accum_out=ssq2[0:rows, part, j:j + 1]).then_inc(ysq_done, 1)

            for r in range(12):
                p = r // 4
                if 0 < r < 11:
                    take_y(act, copy, r)
                if r == 10:
                    y_squares(2, 0)
                elif r % 2 and r != 9:
                    y_squares(p, r % 4 // 2)
                if r % 4 == 3:
                    act.wait_ge(yms_done, p + 1)
                    act.activation(root[:, 3 * p:3 * p + 3], ssq[:, 3 * p:3 * p + 3], ACT.Sqrt).then_inc(yroot_done, 1)

        @block.vector
        def _(dve):
            chain = Chain(dve, dve_step)
            link = chain.link

            def split_lo(half, c1):
                dve.wait_ge(w_hi, c1)
                dve.tensor_tensor(up_lo[:, half], raw[:, half], up_hi[:, half].bitcast(F32), ALU.subtract)\
                    .then_inc(w_lo, 1)

            def x_split(j):
                rows = TILE_ROWS[j]
                dve.wait_ge(x_hi, j + 1)
                col = slice(j * P, j * P + rows)
                dve.tensor_tensor(h_lo[:, :, col], x_banks(j, rows), h_hi[:, :, col].bitcast(F32), ALU.subtract)\
                    .then_inc(x_lo, 1)

            def inverse_root(rows, tiles):
                a, b, c = (t[0:rows, tiles] for t in (rstd, root, ssq))
                link(dve.reciprocal(a, b))
                link(dve.tensor_tensor(b, a, a, ALU.mult))
                link(dve.tensor_tensor(b, b, c, ALU.mult))
                link(dve.tensor_scalar(b, b, -0.5, 1.5, ALU.mult, ALU.add))
                link(dve.tensor_tensor(a, a, b, ALU.mult))

            def x_mean_squares(g):
                tiles = slice(*X_GROUPS[g])
                dve.wait_ge(x_sq, tiles.stop)
                dve.tensor_scalar(ssq[:, tiles], ssq[:, tiles], 1.0 / D, EPS, ALU.mult, ALU.add).then_inc(x_ms, 1)

            def x_inverse(g):
                dve.wait_ge(x_root, g + 1)
                inverse_root(P, slice(*X_GROUPS[g]))

            def x_scale(j):
                rows = TILE_ROWS[j]
                dve.scalar_tensor_tensor(xtok[0:rows, j, :], xtok[0:rows, j, :], rstd[0:rows, j:j + 1],
                                         gmix_b[0:rows, :], ALU.mult, ALU.mult).then_inc(x_scaled, 1)

            x_mean_squares(0)
            x_inverse(0)
            dve.wait_ge(gmix_in, 16)
            x_scale(0)
            x_mean_squares(1)
            x_inverse(1)
            x_scale(1)
            x_scale(2)
            x_split(0)
            x_mean_squares(2)
            x_inverse(2)
            x_scale(3)
            x_split(1)
            x_scale(4)
            x_split(2)
            x_mean_squares(3)
            x_scale(5)
            x_inverse(3)
            x_split(3)
            x_scale(6)
            split_lo(0, 1)
            x_split(4)
            x_scale(7)
            x_split(5)
            x_scale(8)
            for j in range(6, NTILE):
                x_split(j)
            split_lo(1, 2)

            def take(rnd):
                dve.wait_ge(aux_full, rnd + 1)

            def pool_group(g):
                w = 2 << g
                u = uext[:, g, :]
                dve.wait_ge(proj_done, g + 1)
                dve.wait_ge(d_done, g)
                src = u
                for level in range(g + 1):
                    dst = (sum_a, sum_b)[level % 2]
                    lo, step = (2 << level) - 1, 1 << level
                    link(dve.tensor_tensor(dst[:, lo:UEXT], src[:, lo:UEXT], src[:, lo - step:UEXT - step], ALU.add))
                    src = dst
                if g:
                    dve.wait_ge(acc_full, ENTRIES.index(("pool", g - 1)) + 1)
                link(dve.scalar_tensor_tensor(dT[:, 0:SEQ], src[:, PSTATE:PSTATE + SEQ], 1.0 / w,
                                              u[:, PSTATE:PSTATE + SEQ], ALU.mult, ALU.subtract))
                link(dve.tensor_tensor(dT[:, 0:w - 1], src[:, PSTATE:PSTATE + w - 1], rcount[:, 0:w - 1], ALU.mult))
                link(dve.tensor_tensor(dT[:, 0:w - 1], dT[:, 0:w - 1], u[:, PSTATE:PSTATE + w - 1], ALU.subtract))
                dve.scalar_tensor_tensor(dT[:, SEQ:T].rearrange("p (b t) -> p b t", b=DEC_B),
                                         samples(src, USAMP, PSTATE + DEC_T), 1.0 / w,
                                         samples(u, USAMP, PSTATE + DEC_T), ALU.mult, ALU.subtract).then_inc(d_done, 1)

            for f, (kind, n) in enumerate(ENTRIES):
                if f == 0:
                    take(AUX_CONST)
                    dve.tensor_copy(cols[:, :], aux[:, 0:8 * NFF + KD + NG])
                    dve.tensor_copy(smask[:, :], aux[:, 512:512 + SKEYS])
                    dve.tensor_copy(sink_s[:, :], aux[:, 768:770]).then_inc(aux_free, 1)
                elif f == 1:
                    take(AUX_CONV)
                    dve.tensor_copy(cstate[:, :, :], aux[:, 0:2 * NFF * 16].rearrange("p (c s) -> p c s", s=16))\
                        .then_inc(aux_free, 1)
                elif f == 2:
                    take(AUX_POOL)
                    for g in range(NG):
                        dst = uext[:, g, USAMP:UEXT].rearrange("p (b w) -> p b w", b=DEC_B)[:, :, 0:PSTATE]
                        src = aux[:, g * P:g * P + DEC_B * PSTATE].rearrange("p (b w) -> p b w", b=DEC_B)
                        ins = dve.tensor_copy(dst, src)
                    ins.then_inc(aux_free, 1)
                elif f == 3:
                    take(AUX_KC)
                    dve.tensor_copy(kcT[:, :, :], aux[:, :].rearrange("p (b t) -> p b t", b=DEC_B)).then_inc(aux_free, 1)
                elif f == 4:
                    dve.wait_ge(uzero_done, 1)
                    dve.wait_ge(aux_free, AUX_POOL + 1)
                    link(dve.memset(dT[:, PADS], 0.0))
                    pool_group(0)
                elif f == 5:
                    take(AUX_U)
                    dve.tensor_copy(uout_p[0:PSTATE, :], aux[0:PSTATE, 0:POOL_W])
                    dve.tensor_copy(uout_s[0:NSAMP, :], aux[0:NSAMP, 512:1024]).then_inc(aux_free, 1)
                elif f == 12:
                    take(AUX_V)
                    dve.tensor_copy(vtok[:, 1:1 + NBLK, :], aux[:, :].rearrange("p (n d) -> p n d", n=NBLK)).then_inc(aux_free, 1)
                    take(AUX_VNEW)
                    dve.tensor_copy(vnew[0:DEC_T, :, :], aux[0:DEC_T, :].rearrange("p (b d) -> p b d", b=DEC_B))\
                        .then_inc(aux_free, 1)
                if kind == "pool":
                    if n + 1 < NG:
                        pool_group(n + 1)
                else:
                    c = FIRST_CHUNK[kind] + n + 2
                    if f < 12:
                        split_lo(c % 2, c + 1)
            take(AUX_K)
            dve.wait_ge(d_done, NG)
            dve.tensor_copy(kout_p[:, :], aux[:, 0:P])
            dve.tensor_copy(kout_s[0:NSAMP, :], aux[0:NSAMP, 512:512 + P]).then_inc(aux_free, 1)
            split_lo(1, CHUNK_GATE + 2)

            def score_max(rnd, scores, msk, out, sink, g, done):
                dve.wait_ge(aux_full, rnd + 1)
                n = out.shape[-1]
                dve.scalar_tensor_tensor(out, scores, SCALE, msk.unsqueeze(1).to_broadcast([P, g, n]), ALU.mult, ALU.add)\
                    .then_inc(aux_free, 1)
                dve.wait_ge(aux_free, rnd + 1)
                link(dve.tensor_reduce(smx[:, 0:g], out, AX.X, ALU.max))
                link(dve.tensor_tensor(smx[:, 0:g], smx[:, 0:g], sink, ALU.max))
                link(dve.tensor_scalar(snegm[:, 0:g], smx[:, 0:g], -1.0, None, ALU.mult))
                dve.tensor_tensor(sesink[:, 0:g], sink, snegm[:, 0:g], ALU.add).then_inc(done, 1)

            def normalise(out, g, done):
                link(dve.tensor_tensor(sden[:, 0:g], ssum[:, 0:g], sesink[:, 0:g], ALU.add))
                link(dve.reciprocal(srec[:, 0:g], sden[:, 0:g]))
                dve.tensor_tensor(out, out, srec[:, 0:g].unsqueeze(2).to_broadcast([P, g, out.shape[-1]]), ALU.mult)\
                    .then_inc(done, 1)

            def softmax(s, kv, msk):
                score_max(aux_scores(s), aux[:, :].rearrange("p (c n) -> p c n", c=NQ), msk, prob[:, :, :],
                          sink_b[:, kv * NQ:(kv + 1) * NQ], NQ, smax_done)
                dve.wait_ge(exp_done, s + 1)
                normalise(prob[:, :, :], NQ, prob_done)

            def take_values(n, kv):
                v = slice(kv * HD, (kv + 1) * HD)
                dve.wait_ge(aux_full, aux_values(n * 2 + kv) + 1)
                dve.tensor_copy(qT[v, :, bass.ds(n * WIN, WIN)], aux[v, 0:NQ * P].rearrange("p (c t) -> p c t", c=NQ))\
                    .then_inc(aux_free, 1)

            def take_probs(s):
                dve.wait_ge(aux_full, aux_turn(s) + 1)
                dve.tensor_copy(probT[:, :, :], aux[:, :].rearrange("p (b n) -> p b n", b=2)).then_inc(aux_free, 1)

            def sample_part(h):
                r_s, r_t, r_v = AUX_SAMPLE[h]
                banks = aux[:, :].rearrange("p (v n) -> p v n", v=2)
                score_max(r_s, banks[:, :, 0:SKEYS], smask[:, :], sprob[:, :, :], sink_s[:, :], 2, ssmax_done)
                take_probs(h)
                if h:
                    split_lo(0, CHUNK_GATE + 3)
                take_values(0, h)
                dve.wait_ge(sexp_done, h + 1)
                normalise(sprob[:, :, :], 2, sprob_done)
                take(r_t)
                dve.tensor_copy(sprob_c[:, :, :], banks[:, :, 0:P])
                dve.tensor_copy(sprob_n[0:DEC_T, :, :], banks[0:DEC_T, :, P:2 * P]).then_inc(aux_free, 1)
                take(r_v)
                for kv in range(2):
                    v = slice(kv * HD, (kv + 1) * HD)
                    for i in range(4):
                        col = SEQ + (4 * h + i) * DEC_T
                        ins = dve.tensor_copy(qT[v, :, col:col + DEC_T],
                                              banks[v, kv, 32 * i:32 * i + 32].rearrange("p (c t) -> p c t", c=NQ))
                ins.then_inc(aux_free, 1)

            def branch_input_low(k):
                dve.wait_ge(ao_hi_done, k + 1)
                dve.tensor_tensor(ao_lo[:, k, :], uext[:, k, 0:TP] if k < 4 else qT[:, k - 4, :],
                                  ao_hi[:, k, :].bitcast(F32), ALU.subtract).then_inc(ao_lo_done, 1)

            def gate_block(n, first, last):
                for kv in range(2):
                    if first:
                        sample_part(kv)
                    else:
                        take_probs(n * 2 + kv)
                        split_lo(1 - kv, n * 2 + (CHUNK_GATE + 2 + kv))
                        if last and kv:
                            branch_input_low(0)
                            branch_input_low(1)
                        take_values(n, kv)
                    if not (last and kv):
                        softmax(n * 2 + (kv + 1), (kv + 1) % 2, (mask_first if first and kv == 0 else mask)[:, :])

            dve.wait_ge(u_out, 16 * 9)
            softmax(0, 0, mask_first[:, :])
            gate_block(0, True, False)
            with dve.Fori(0, 6) as i:
                chain.enter(i, 10)
                gate_block(i + 1, False, False)
            chain.leave(6, 10)
            gate_block(7, False, True)

            for k in range(2, KD):
                branch_input_low(k)
                if k == 4:
                    split_lo(1, CHUNK_BRANCH + 2)

            def mix(m, half):
                dve.wait_ge(gate_in[half], (m - half) * 16 + 32)
                for b in range(2):
                    dve.wait_ge(acc_full, m * 2 + (FILL_BRANCH + b + 1))
                    g = pieces(gates[:, half, b, :])
                    dve.tensor_tensor(g, acc[b], g, ALU.mult).then_inc(acc_free, 1)
                dve.wait_ge(acc_free, m * 2 + 2)
                dve.tensor_tensor(gates[:, half, 0, :], gates[:, half, 0, :], gates[:, half, 1, :], ALU.add)\
                    .then_inc(mix_sum, 1)
                split_lo(half, m + (CHUNK_BRANCH + 3))
                dve.wait_ge(mix_hi_done, m + 1)
                dve.tensor_tensor(mx_lo[:, bass.ds(m, 1), :], gates[:, half, 0:1, :],
                                  mx_hi[:, bass.ds(m, 1), :].bitcast(F32), ALU.subtract).then_inc(mix_lo_done, 1)

            with dve.Fori(0, 4) as i:
                for half in range(2):
                    mix(i * 2 + half, half)

            def project(m, half):
                dve.wait_ge(aux_free, m * 2 + (AUX_X + 2))
                dve.wait_ge(acc_full, m + (FILL_OUT + 1))
                dve.tensor_tensor(y[:, bass.ds(m, 1), :].rearrange("p o (a n) -> p (o a) n", a=3), acc[half],
                                  pieces(xT[:, half, :]), ALU.add).then_inc(acc_free, 1)
                split_lo(half, m + (CHUNK_OUT + 3))

            with dve.Fori(0, 3) as i:
                for half in range(2):
                    project(i * 2 + half, half)
            project(KD - 2, 0)

            def ffn_input_low(k):
                dve.wait_ge(h2_hi_done, k + 1)
                dve.scalar_tensor_tensor(h2_lo[:, k, :], y[:, k, :], gffn[:, k:k + 1], h2_hi[:, k, :].bitcast(F32),
                                         ALU.mult, ALU.subtract).then_inc(h2_lo_done, 1)

            for k in range(KD - 2):
                ffn_input_low(k)
            project(KD - 1, 1)
            ffn_input_low(KD - 2)
            ffn_input_low(KD - 1)

            def mean_squares(rnd):
                take(rnd)
                dve.tensor_scalar(ssq[:, 0:NTILE - 1], aux[:, 0:NTILE - 1], 1.0 / D, EPS, ALU.mult, ALU.add)
                dve.tensor_scalar(ssq[0:NSAMP, NTILE - 1:NTILE], aux[0:NSAMP, NTILE - 1:NTILE], 1.0 / D, EPS,
                                  ALU.mult, ALU.add).then_inc(aux_free, 1)

            mean_squares(AUX_SSQ)
            dve.wait_ge(root2, 1)
            inverse_root(P, slice(0, NTILE))
            for j in range(NTILE):
                ins = dve.tensor_scalar(diag[:, j, :], ident[:, :], rstd[:, j:j + 1], None, ALU.mult)
            ins.then_inc(diag_done, 1)
            take(AUX_RMS)
            dve.tensor_copy(rms_row[:, 0:SEQ], aux[:, 0:SEQ]).then_inc(aux_free, 1)
            take(AUX_RMS + 1)
            dve.tensor_copy(rms_row[:, SEQ:T], aux[:, 0:NSAMP]).then_inc(aux_free, 1)
            dve.wait_ge(aux_free, AUX_RMS + 2)

            def scale_up(s, fill, val, u, first=False):
                dve.wait_ge(acc_full, fill)
                if not first:
                    dve.wait_ge(conv_done, u)
                    dve.wait_ge(tails_taken, u - 1)
                ext = ext_val if val else ext_gate
                dve.tensor_tensor(ext[:, CSTATE:CSTATE + 2 * NP].rearrange("p (a n) -> p a n", a=2), acc[s][:, 0:2, :],
                                  rms_row[:, 0:2 * NP].rearrange("p (a n) -> p a n", a=2), ALU.mult)
                dve.tensor_tensor(ext[:, CSTATE + 2 * NP:CSTATE + SEQ], acc[s][:, 2, 0:SEQ - 2 * NP],
                                  rms_row[:, 2 * NP:SEQ], ALU.mult)
                dve.tensor_tensor(samples(ext, ESAMP, CSTATE + DEC_T),
                                  acc[s][:, 2, SEQ - 2 * NP:T - 2 * NP].rearrange("p (b t) -> p b t", b=DEC_B),
                                  rms_row[:, SEQ:T].rearrange("p (b t) -> p b t", b=DEC_B), ALU.mult)\
                    .then_inc(up_scaled, 1)

            def conv(u1, ch, val, steps=(0, 1, 2)):
                ext, dst = (ext_val, conv_val) if val else (ext_gate, conv_gate)

                def tap(a):
                    return cw[:, a, bass.ds(ch, 1)]
                if 0 in steps:
                    dve.wait_ge(up_scaled, u1)
                    dve.wait_ge(states_in, u1)
                    link(dve.tensor_scalar(dst[:, 0:NCONV], ext[:, 2:EXT], tap(2), tap(3), ALU.mult, ALU.add))
                if 1 in steps:
                    link(dve.scalar_tensor_tensor(dst[:, 0:NCONV], ext[:, 1:EXT - 1], tap(1), dst[:, 0:NCONV],
                                                  ALU.mult, ALU.add))
                if 2 in steps:
                    dve.scalar_tensor_tensor(dst[:, 0:NCONV], ext[:, 0:NCONV], tap(0), dst[:, 0:NCONV],
                                             ALU.mult, ALU.add).then_inc(conv_done, 1)

            def product(j, u1):
                dve.wait_ge(silu_done, j + 1)
                dve.wait_ge(conv_done, u1)
                dve.tensor_tensor(conv_val[:, 0:NCONV], conv_val[:, 0:NCONV], conv_gate[:, 0:NCONV], ALU.mult)\
                    .then_inc(prod_done, 1)

            def act_low(j, e):
                dve.wait_ge(act_hi_done, j + 1)
                dve.tensor_tensor(act_lo[:, e, 0:SEQ], conv_val[:, 0:SEQ], act_hi[:, e, 0:SEQ].bitcast(F32), ALU.subtract)
                dve.tensor_tensor(act_lo[:, e, SEQ:T].rearrange("p (b t) -> p b t", b=DEC_B),
                                  samples(conv_val, ESAMP - CSTATE, CSTATE + DEC_T),
                                  act_hi[:, e, SEQ:T].bitcast(F32).rearrange("p (b t) -> p b t", b=DEC_B),
                                  ALU.subtract).then_inc(act_lo_done, 1)

            scale_up(0, FILL_FFN + 1, 0, 0, first=True)
            conv(1, 0, 0)
            split_lo(0, CHUNK_UP + 3)

            def ffn(i, last):
                fill = i * 12 + FILL_FFN
                scale_up(1, fill + 2, 1, i * 4 + 1)
                conv(i * 4 + 2, i * 2 + NFF, 1)
                product(i * 2, i * 4 + 2)
                split_lo(1, i * 4 + (CHUNK_UP + 4))
                dve.wait_ge(dn_hi_done, i + 1)
                dve.tensor_tensor(dn_lo[:, :, :], raw_dn[:, :, :], dn_hi[:, :, :].bitcast(F32), ALU.subtract)\
                    .then_inc(dn_lo_done, 1)
                act_low(i * 2, 0)
                scale_up(0, fill + 3, 0, i * 4 + 2)
                conv(i * 4 + 3, i * 2 + 1, 0)
                if not last:
                    split_lo(0, i * 4 + (CHUNK_UP + 5))
                if last:
                    return
                scale_up(1, fill + 4, 1, i * 4 + 3)
                conv(i * 4 + 4, i * 2 + (NFF + 1), 1)
                product(i * 2 + 1, i * 4 + 4)
                split_lo(1, i * 4 + (CHUNK_UP + 6))
                act_low(i * 2 + 1, 1)
                scale_up(0, fill + 5, 0, i * 4 + 4)
                for m in range(KD):
                    dve.wait_ge(acc_free, i * 8 + (FILL_FFN - FILL_BRANCH + m - 7))
                    dve.wait_ge(acc_full, i * 12 + (FILL_FFN + 6 + m))
                    dve.tensor_tensor(pieces(y[:, m, :]), acc[1 - m % 2], pieces(y[:, m, :]), ALU.add).then_inc(acc_free, 1)
                    if m < 3:
                        conv(i * 4 + 5, i * 2 + 2, 0, steps=(m,))
                    if m == 3:
                        split_lo(0, i * 4 + (CHUNK_UP + 7))

            with hinted_loop(mybir.EngineType.DVE, NFF // 2 - 1) as i:
                chain.enter(i, 8)
                ffn(i, False)
            chain.leave(NFF // 2 - 1, 8)
            i = NFF // 2 - 1
            ffn(i, True)

            def seg_scale(p):
                first, width = SEGS[p]
                if p == 0:
                    dve.wait_ge(acc_full, i * 12 + (FILL_FFN + 4))
                    dve.wait_ge(conv_done, i * 4 + 3)
                    dve.wait_ge(tails_taken, i * 4 + 2)
                bank = PS[:, 3 + p, :]
                n = min(width, SEQ - first)
                ins = dve.tensor_tensor(ext_val[:, CSTATE + first:CSTATE + first + n], bank[:, 0:n],
                                        rms_row[:, first:first + n], ALU.mult)
                if p == 2:
                    ins = dve.tensor_tensor(samples(ext_val, ESAMP, CSTATE + DEC_T),
                                            bank[:, n:width].rearrange("p (b t) -> p b t", b=DEC_B),
                                            rms_row[:, SEQ:T].rearrange("p (b t) -> p b t", b=DEC_B), ALU.mult)
                ins.then_inc(seg_scaled, 1)

            def seg_convolve(p):
                first = SEGS[p][0]
                n = SEG if p < 2 else NCONV - first
                out = conv_val[:, first:first + n]

                def tap(a):
                    return cw[:, a, 2 * NFF - 1:2 * NFF]
                dve.wait_ge(seg_scaled, p + 1)
                dve.wait_ge(states_in, i * 4 + 4)
                link(dve.tensor_scalar(out, ext_val[:, first + 2:first + n + 2], tap(2), tap(3), ALU.mult, ALU.add))
                link(dve.scalar_tensor_tensor(out, ext_val[:, first + 1:first + n + 1], tap(1), out, ALU.mult, ALU.add))
                link(dve.scalar_tensor_tensor(out, ext_val[:, first:first + n], tap(0), out, ALU.mult, ALU.add))

            def seg_product(p):
                first = SEGS[p][0]
                n = SEG if p < 2 else NCONV - first
                dve.wait_ge(silu_done, i * 2 + 2)
                out = conv_val[:, first:first + n]
                dve.tensor_tensor(out, out, conv_gate[:, first:first + n], ALU.mult).then_inc(seg_prod, 1)

            def seg_low(p):
                first, width = SEGS[p]
                n = min(width, SEQ - first)
                dve.wait_ge(seg_hi, p + 1)
                ins = dve.tensor_tensor(act_lo[:, 1, first:first + n], conv_val[:, first:first + n],
                                        act_hi[:, 1, first:first + n].bitcast(F32), ALU.subtract)
                if p == 2:
                    ins = dve.tensor_tensor(act_lo[:, 1, SEQ:T].rearrange("p (b t) -> p b t", b=DEC_B),
                                            samples(conv_val, ESAMP - CSTATE, CSTATE + DEC_T),
                                            act_hi[:, 1, SEQ:T].bitcast(F32).rearrange("p (b t) -> p b t", b=DEC_B),
                                            ALU.subtract)
                ins.then_inc(seg_lo, 1)

            def add_fill(f):
                first, width = SEGS[f // KD]
                rows = y[:, f % KD, first:first + width]
                dve.wait_ge(sums_full, f + 1)
                dve.tensor_tensor(rows, PS[:, f % 6, 0:width], rows, ALU.add).then_inc(sums_added, 1)

            def final_rms(p):
                tiles = slice(3 * p, 3 * p + 3)
                dve.wait_ge(ysq_done, 6 * p + 6)
                link(dve.tensor_tensor(ssq[:, tiles], ssq2[:, 0, tiles], ssq2[:, 1, tiles], ALU.add))
                dve.tensor_scalar(ssq[:, tiles], ssq[:, tiles], 1.0 / D, EPS, ALU.mult, ALU.add).then_inc(yms_done, 1)
                dve.wait_ge(yroot_done, p + 1)
                inverse_root(P, tiles)

            def final_scale(j):
                rows = TILE_ROWS[j]
                if j == 0:
                    dve.wait_ge(gfin_in, 16)
                dve.scalar_tensor_tensor(ytok[0:rows, j, :], ytok[0:rows, j, :], rstd[0:rows, j:j + 1],
                                         gfin_b[0:rows, :], ALU.mult, ALU.mult).then_inc(y_scaled, 1)

            seg_scale(0)
            seg_convolve(0)
            seg_scale(1)
            seg_product(0)
            seg_scale(2)
            seg_low(0)
            seg_convolve(1)
            seg_product(1)
            dve.wait_ge(acc_free, FILL_FFN - FILL_BRANCH + 8 * i)
            add_fill(0)
            seg_low(1)
            add_fill(1)
            seg_convolve(2)
            add_fill(2)
            seg_product(2)
            add_fill(3)
            seg_low(2)
            for f in range(4, 3 * KD):
                add_fill(f)
                p, m = f // KD - 1, f % KD
                if p >= 0 and m == 4:
                    final_rms(p)
                if p >= 0 and m >= 5 and f < 3 * KD - 2:
                    final_scale(3 * p + m - 5)
            final_scale(4)
            take_y(dve, dve.tensor_copy, 11)
            final_scale(5)
            final_rms(2)
            dve.wait_ge(aux_free, AUX_Y + 12)
            for j in range(6, NTILE):
                final_scale(j)

        @block.gpsimd
        def _(pool):
            chain = Chain(pool, pool_step)
            link = chain.link

            def select(t, compare, fill, base, pattern, mult):
                return pool.affine_select(out=t, in_=t, compare_op=compare, fill=fill, base=base, pattern=pattern,
                                          channel_multiplier=mult)

            pool.memset(ident[:, :], 0.0)
            pool.memset(ssq[:, :], 1.0)
            link(pool.memset(ones[:, :], 1.0))
            select(ident[:, :], ALU.not_equal, 1.0, 0, [[-1, P]], 1).then_inc(const_done, 1)

            for t in (h_hi, h_lo):
                pool.memset(t[:, :, PADS].bitcast(F32), 0.0)
            pool.memset(kT[:, 0:WIN], 0.0)
            pool.memset(rep8[0:8, :, :], 0.0)
            pool.memset(rep4[0:4, :, :, :], 0.0)
            pool.memset(mask8[0:8, :], 0.0)
            pool.memset(mask[:, :], 0.0)
            for t in range(PSTATE):
                pool.memset(rcount[:, t:t + 1], 1.0 / (t + 1))
            link(pool.memset(mask_first[:, 0:WIN], MASKED))
            select(rep8[0:8], ALU.not_equal, 1.0, 0, [[0, 16], [1, 8]], -1)
            select(rep4[0:4], ALU.not_equal, 1.0, 0, [[0, 4], [1, 4], [0, 8]], -1)
            link(select(mask8[0:8, :], ALU.is_ge, MASKED, 0, [[1, SKEYS]], -1))
            select(mask8[0:8, :], ALU.is_ge, MASKED, WIN, [[-1, SKEYS]], 1)
            link(select(mask[:, :], ALU.is_ge, MASKED, 0, [[1, 2 * WIN]], -1))
            link(select(mask[:, :], ALU.is_ge, MASKED, WIN, [[-1, 2 * WIN]], 1))
            pool.tensor_copy(mask_first[:, WIN:2 * WIN], mask[:, WIN:2 * WIN]).then_inc(const_done, 1)
            pool.wait_ge(xt_full, NTILE)
            pool.memset(uext[:, :, 0:PSTATE], 0.0).then_inc(uzero_done, 1)
            pool.wait_ge(aux_full, AUX_CONST + 1)
            link(pool.memset(vtok[:, 0, :], 0.0))
            pool.wait_ge(proj_done, 4)
            for g in range(NG):
                ins = pool.tensor_copy(upack[:, g, :].rearrange("p (b t) -> p b t", b=DEC_B),
                                       samples(uext[:, g, :], USAMP, PSTATE + DEC_T))
            ins.then_inc(u_packed, 1)

            def stage_qk(n, rnd):
                pool.wait_ge(aux_full, rnd + 1)
                pool.wait_ge(uzero_done, 1)
                pool.tensor_copy(qblk[:, :, :], qT[:, :, bass.ds(n * WIN, WIN)])
                pool.tensor_copy(kblk[:, :], kT[:, bass.ds(n * WIN, 2 * WIN)]).then_inc(qk_staged, 1)

            def stage_v(n, rnd):
                if rnd is not None:
                    pool.wait_ge(aux_full, rnd + 1)
                    pool.wait_ge(const_done, 2)
                pool.tensor_copy(vblk[:, :, :], vtok[:, bass.ds(n, 2), :]).then_inc(v_staged, 1)

            pool.wait_ge(proj_done, 11)
            for b in range(DEC_B):
                pool.tensor_copy(qpack[:, b, :, :], qT[:, :, SEQ + b * DEC_T:SEQ + (b + 1) * DEC_T])
            pool.tensor_copy(qblk[:, :, :], qT[:, :, 0:WIN])
            pool.wait_ge(proj_done, 13)
            pool.tensor_copy(kblk[:, :], kT[:, 0:2 * WIN]).then_inc(qk_staged, 1)
            pool.wait_ge(aux_free, AUX_V + 1)
            stage_v(0, None)
            stage_qk(1, aux_scores(1))
            stage_v(1, aux_values(1))
            with pool.Fori(0, 6) as i:
                stage_qk(i + 2, aux_scores(i * 2 + 3))
                stage_v(i + 2, aux_values(i * 2 + 3))

            pool.wait_ge(acc_full, FILL_OUT)
            pool.memset(ext_gate[:, 0:CSTATE], 0.0)
            pool.memset(ext_val[:, 0:CSTATE], 0.0)
            pool.memset(xT[:, :, PADS], 0.0)
            pool.memset(ssq2[:, :, :], 1.0)
            pool.memset(sqsum[:, :], 0.0).then_inc(pads_done, 1)
            pool.wait_ge(pads_done, 1)

            def add_squares(m, total, square):
                pool.wait_ge(sq_added, m)
                pool.wait_ge(sq_done, m + 1)
                pool.tensor_tensor(total[:, :], total[:, :], square[:, :], ALU.add).then_inc(sq_added, 1)

            with pool.Fori(0, KD) as m:
                add_squares(m, sqsum, sq)

            pool.wait_ge(aux_full, AUX_SSQ + 1)
            for t in (act_hi, act_lo):
                ins = pool.memset(t[:, :, PADS].bitcast(F32), 0.0)
            ins.then_inc(pads_done, 1)


_INS = ["x_prompt", "x_sample", "state_pool", "cache_k", "cache_v", "state_conv", "g_mix", "w_in", "w_pool_grp",
        "pool_scale", "sinks", "w_branch_pool", "w_branch_attn", "w_out", "g_ffn", "w_up", "conv_w", "conv_b",
        "w_down", "g_final"]
_OUTS = [(1, SEQ, D), (DEC_B, DEC_T, D), (1, 1, PSTATE, POOL_W), (1, 1, WIN, 2, HD), (1, 1, WIN, 2, HD),
         (1, 1, CSTATE, 2 * D_FF), (1, DEC_B, PSTATE, POOL_W), (1, DEC_B, WIN, 2, HD), (1, DEC_B, WIN, 2, HD),
         (1, DEC_B, CSTATE, 2 * D_FF)]


def kernel(**inputs):
    import numpy as _np
    import concourse.bacc as _bacc
    from concourse import mybir as _mybir
    from concourse.bass_utils import run_bass_kernel_spmd as _run

    nc = _bacc.Bacc("TRN2", target_bir_lowering=False, num_devices=1)
    arrays, args = {}, []
    for name in _INS:
        a = _np.ascontiguousarray(inputs[name])
        arrays[f"in_{name}_dram"] = a
        args.append(nc.dram_tensor(f"in_{name}_dram", a.shape, _mybir.dt.from_np(a.dtype), kind="ExternalInput").ap())
    for i, shape in enumerate(_OUTS):
        args.append(nc.dram_tensor(f"out_{i}_dram", shape, _mybir.dt.float32, kind="ExternalOutput").ap())
    hybrid_layer(nc, *args)
    r = _run(nc, [arrays], core_ids=[0])
    return tuple(r.results[0][f"out_{i}_dram"] for i in range(len(_OUTS)))
```
